# Optimizing a Trainium2 kernel written in Bass

```python
import jax, jax.numpy as jnp
from jax import lax
import numpy as np

D_MODEL = 1024
BATCH = 1
SEQ = 4096
DEPTH = 1

CHUNK = 64
EPS = 1e-6

DN_HEADS = 4
DN_HEAD_DIM = 128
DN_WIDTH = DN_HEADS * DN_HEAD_DIM
CONV_K = 4

SW_HEADS = 8
SW_KV_HEADS = 2
SW_GROUP = SW_HEADS // SW_KV_HEADS
SW_HEAD_DIM = 64
SW_WIDTH = SW_HEADS * SW_HEAD_DIM
SW_KV_WIDTH = SW_KV_HEADS * SW_HEAD_DIM
WINDOW = 128
WINDOW_CHUNKS = WINDOW // CHUNK
ROPE_THETA = 10000.0

D_MIX = DN_WIDTH + SW_WIDTH
IN_SPLITS = (DN_WIDTH, DN_WIDTH, DN_WIDTH, DN_WIDTH, DN_HEADS, DN_HEADS,
             SW_WIDTH, SW_KV_WIDTH, SW_KV_WIDTH, SW_WIDTH)
IN_COLS = int(sum(IN_SPLITS))
IN_OFFSETS = [int(o) for o in np.cumsum(IN_SPLITS)[:-1]]

kernel_name = "hybrid_gated_deltanet_swa_sink_sandwich"

def rmsnorm(x, w):
    xf = x.astype(jnp.float32)
    y = xf * lax.rsqrt(jnp.mean(xf * xf, axis=-1, keepdims=True) + EPS)
    return (y * w.astype(jnp.float32)).astype(x.dtype)

def l2norm(x):
    return x * lax.rsqrt(jnp.sum(x * x, axis=-1, keepdims=True) + EPS)

def causal_depthwise_conv(x, w):
    s = x.shape[1]
    xp = jnp.pad(x, ((0, 0), (CONV_K - 1, 0), (0, 0)))
    out = xp[:, 0:s] * w[0]
    for i in range(1, CONV_K):
        out = out + xp[:, i:i + s] * w[i]
    return out

def rope(x, pos):
    d = x.shape[-1]
    half = d // 2
    inv_freq = ROPE_THETA ** (-jnp.arange(half, dtype=jnp.float32) * 2.0 / d)
    ang = pos[:, None] * inv_freq[None, :]
    cos = jnp.cos(ang)[None, :, None, :]
    sin = jnp.sin(ang)[None, :, None, :]
    x1, x2 = x[..., :half], x[..., half:]
    return jnp.concatenate([x1 * cos - x2 * sin, x2 * cos + x1 * sin], axis=-1)

def gated_deltanet(q, k, v, a, b, a_log, dt_bias):
    bsz, s, h, d = q.shape
    n = s // CHUNK
    q = l2norm(q) * (d ** -0.5)
    k = l2norm(k)
    beta = jax.nn.sigmoid(b)
    g = -jnp.exp(a_log) * jax.nn.softplus(a + dt_bias)

    def to_chunks(t):
        t = t.reshape((bsz, n, CHUNK, h) + t.shape[3:])
        return jnp.moveaxis(t, 3, 1)

    qc, kc, vc = to_chunks(q), to_chunks(k), to_chunks(v)
    bc, gc = to_chunks(beta), to_chunks(g)
    G = jnp.cumsum(gc, axis=-1)
    causal = jnp.tril(jnp.ones((CHUNK, CHUNK), dtype=bool))
    strict = jnp.tril(jnp.ones((CHUNK, CHUNK), dtype=bool), k=-1)
    decay = jnp.exp(jnp.where(causal, G[..., :, None] - G[..., None, :], -jnp.inf))

    k_beta = kc * bc[..., None]
    v_beta = vc * bc[..., None]
    lower = jnp.where(strict, jnp.einsum('bhnid,bhnjd->bhnij', k_beta, kc) * decay, 0.0)
    eye = jnp.eye(CHUNK, dtype=jnp.float32)
    rhs = jnp.concatenate([v_beta, k_beta * jnp.exp(G)[..., None]], axis=-1)
    sol = lax.linalg.triangular_solve(eye + lower, rhs, left_side=True, lower=True,
                                      unit_diagonal=True)
    value, k_cum = sol[..., :d], sol[..., d:]

    attn_intra = jnp.einsum('bhnid,bhnjd->bhnij', qc, kc) * decay
    q_exp = qc * jnp.exp(G)[..., None]
    k_tail = kc * jnp.exp(G[..., -1:] - G)[..., None]
    g_last = jnp.exp(G[..., -1])

    xs = tuple(jnp.moveaxis(t, 2, 0) for t in (q_exp, k_cum, value, attn_intra, k_tail, g_last))

    def step(state, inp):
        qe, kcu, val, ai, kt, gl = inp
        v_new = val - jnp.einsum('bhcd,bhde->bhce', kcu, state)
        o = jnp.einsum('bhcd,bhde->bhce', qe, state) + jnp.einsum('bhij,bhje->bhie', ai, v_new)
        state = state * gl[..., None, None] + jnp.einsum('bhcd,bhce->bhde', kt, v_new)
        return state, o

    s0 = jnp.zeros((bsz, h, d, d), jnp.float32)
    _, o = lax.scan(step, s0, xs)
    o = jnp.transpose(o, (1, 0, 3, 2, 4))
    return o.reshape(bsz, s, h, d)

def sliding_window_sink_attention(q, k, v, sinks):
    bsz, s = q.shape[0], q.shape[1]
    n = s // CHUNK
    qc = q.reshape(bsz, n, CHUNK, SW_KV_HEADS, SW_GROUP, SW_HEAD_DIM)
    kc = k.reshape(bsz, n, CHUNK, SW_KV_HEADS, SW_HEAD_DIM)
    vc = v.reshape(bsz, n, CHUNK, SW_KV_HEADS, SW_HEAD_DIM)
    k_blocks, v_blocks, valid = [], [], []
    chunk_idx = jnp.arange(n)
    for j in range(WINDOW_CHUNKS - 1, -1, -1):
        pad = ((0, 0), (j, 0), (0, 0), (0, 0), (0, 0))
        k_blocks.append(jnp.pad(kc, pad)[:, :n])
        v_blocks.append(jnp.pad(vc, pad)[:, :n])
        valid.append(jnp.broadcast_to((chunk_idx - j >= 0)[:, None], (n, CHUNK)))
    kw = jnp.concatenate(k_blocks, axis=2)
    vw = jnp.concatenate(v_blocks, axis=2)
    mask = jnp.concatenate(valid, axis=1)
    scores = jnp.einsum('bnqhgd,bnkhd->bnhgqk', qc, kw) * (SW_HEAD_DIM ** -0.5)
    scores = jnp.where(mask[None, :, None, None, None, :], scores, -jnp.inf)
    sink = jnp.broadcast_to(sinks.reshape(1, 1, SW_KV_HEADS, SW_GROUP, 1, 1),
                            scores.shape[:-1] + (1,))
    p = jax.nn.softmax(jnp.concatenate([scores, sink], axis=-1), axis=-1)[..., :-1]
    out = jnp.einsum('bnhgqk,bnkhd->bnqhgd', p, vw)
    return out.reshape(bsz, s, SW_WIDTH)

def setup_inputs(seed: int = 0) -> dict:
    key = jax.random.key(seed)
    ks = jax.random.split(key, 12)
    x = jax.random.normal(ks[0], (BATCH, SEQ, D_MODEL), jnp.float32)
    pre_norm_w = 1.0 + 0.05 * jax.random.normal(ks[1], (DEPTH, D_MODEL), jnp.float32)
    w_in = jax.random.normal(ks[2], (DEPTH, D_MODEL, IN_COLS), jnp.float32) * D_MODEL ** -0.5
    conv_w = jax.random.normal(ks[3], (DEPTH, CONV_K, 3 * DN_WIDTH), jnp.float32) * CONV_K ** -0.5
    a_init = jax.random.uniform(ks[4], (DEPTH, DN_HEADS), jnp.float32, 1.0, 16.0)
    dn_a_log = jnp.log(a_init)
    dt = jnp.exp(jax.random.uniform(ks[5], (DEPTH, DN_HEADS), jnp.float32,
                                    np.log(1e-3), np.log(1e-1)))
    dn_dt_bias = dt + jnp.log(-jnp.expm1(-dt))
    dn_out_norm_w = 1.0 + 0.05 * jax.random.normal(ks[6], (DEPTH, DN_HEAD_DIM), jnp.float32)
    sw_sinks = 0.5 * jax.random.normal(ks[7], (DEPTH, SW_HEADS), jnp.float32)
    w_out = jax.random.normal(ks[8], (DEPTH, D_MIX, D_MODEL), jnp.float32) * D_MIX ** -0.5
    post_norm_w = 1.0 + 0.05 * jax.random.normal(ks[9], (DEPTH, D_MODEL), jnp.float32)
    return {"x": x, "pre_norm_w": pre_norm_w, "w_in": w_in, "conv_w": conv_w,
            "dn_a_log": dn_a_log, "dn_dt_bias": dn_dt_bias, "dn_out_norm_w": dn_out_norm_w,
            "sw_sinks": sw_sinks, "w_out": w_out, "post_norm_w": post_norm_w}

def reference(x, pre_norm_w, w_in, conv_w, dn_a_log, dn_dt_bias, dn_out_norm_w,
              sw_sinks, w_out, post_norm_w):
    bsz, s, _ = x.shape
    pos = jnp.arange(s, dtype=jnp.float32)
    for l in range(DEPTH):
        h = rmsnorm(x, pre_norm_w[l])
        proj = jnp.einsum('bsd,de->bse', h, w_in[l])
        (qa, ka, va, za, ba, aa, qb, kb, vb, zb) = jnp.split(proj, IN_OFFSETS, axis=-1)

        qkv = jax.nn.silu(causal_depthwise_conv(jnp.concatenate([qa, ka, va], axis=-1), conv_w[l]))
        qkv = qkv.astype(jnp.float32).reshape(bsz, s, 3, DN_HEADS, DN_HEAD_DIM)
        o_a = gated_deltanet(qkv[:, :, 0], qkv[:, :, 1], qkv[:, :, 2],
                             aa.astype(jnp.float32), ba.astype(jnp.float32),
                             dn_a_log[l].astype(jnp.float32), dn_dt_bias[l].astype(jnp.float32))
        o_a = rmsnorm(o_a, dn_out_norm_w[l]).reshape(bsz, s, DN_WIDTH)
        o_a = o_a.astype(x.dtype) * jax.nn.silu(za)

        qh = rope(qb.astype(jnp.float32).reshape(bsz, s, SW_HEADS, SW_HEAD_DIM), pos)
        kh = rope(kb.astype(jnp.float32).reshape(bsz, s, SW_KV_HEADS, SW_HEAD_DIM), pos)
        vh = vb.astype(jnp.float32).reshape(bsz, s, SW_KV_HEADS, SW_HEAD_DIM)
        o_b = sliding_window_sink_attention(qh, kh, vh, sw_sinks[l].astype(jnp.float32))
        o_b = o_b.astype(x.dtype) * jax.nn.silu(zb)

        y = jnp.einsum('bse,ed->bsd', jnp.concatenate([o_a, o_b], axis=-1), w_out[l])
        x = x + rmsnorm(y, post_norm_w[l])
    return x


_drawn_inputs = setup_inputs


def setup_inputs(seed=0):
    import zlib

    import numpy as np

    out = dict(_drawn_inputs(seed))
    spreads = {}
    factors = {'sw_sinks': 64.0}
    for name, (base, spread) in spreads.items():
        noise = np.random.default_rng([zlib.crc32(name.encode()), seed]).standard_normal(out[name].shape)
        drawn = base * np.exp(spread * noise) if base else spread * noise
        out[name] = __import__('jax').numpy.asarray(drawn.astype(out[name].dtype))
    for name, factor in factors.items():
        out[name] = (out[name] * factor).astype(out[name].dtype)
    return out
```

```python
from contextlib import ExitStack

import concourse.bass as bass
from concourse import mybir

ALU = mybir.AluOpType
ACT = mybir.ActivationFunctionType
AX_X = mybir.AxisListType.X
F32 = mybir.dt.float32
F16 = mybir.dt.float16
I32 = mybir.dt.int32
RMAX = bass.bass_isa.ReduceOp.max

TOK = 128
CHUNK = 64
EPS = 1e-6
DN_HEADS = 4
SW_HEADS = 8
DH_B = 64
LEVELS = 7
GATE_LINKS = 15
NEG = -1e30
X_SCALE = 2.0 ** 10
SERIES = [1.0 / (2 * n + 1) for n in range(8)]

COL_Q, COL_K, COL_V, COL_ZA, COL_ZB, COL_QB, COL_KVB = 0, 512, 1024, 1536, 2048, 2560, 3072
FILL_ZA, FILL_V, FILL_KVB, FILL_QB, FILL_ZB, FILL_K, FILL_Q = range(7)
FILL_COL = {FILL_ZA: COL_ZA, FILL_V: COL_V, FILL_ZB: COL_ZB, FILL_K: COL_K, FILL_Q: COL_Q}
PIECES = [(f, b) for f in range(7) for b in range({FILL_KVB: 2}.get(f, 4))]
GROUP = {FILL_Q: 0, FILL_K: 1, FILL_V: 2}


class Nth:

    def __init__(self, sem, per, at):
        self.sem, self.per, self.at = sem, per, at


def done(eng, event, tile):
    if isinstance(tile, int) and tile < 0:
        return
    if isinstance(event, Nth):
        eng.wait_ge(event.sem, tile * event.per + (event.at + 1))
    else:
        eng.wait_ge(event, tile + 1)


def build(nc, x, pre_norm_w, w_in, conv_w, dn_a_log, dn_dt_bias, dn_out_norm_w, sw_sinks, w_out,
          post_norm_w, const32, const16, rotary, out):
    _, SEQ, D = x.shape
    COLS = w_in.shape[2]
    NT = SEQ // TOK
    NC = D // 128
    KV = COLS - COL_KVB
    assert NT % 2 == 0 and COL_KVB + KV == COLS

    with ExitStack() as ctx:
        def sb(name, shape, dt=F32):
            return ctx.enter_context(nc.sbuf_tensor(name, shape, dt))

        def sem(name):
            return ctx.enter_context(nc.semaphore(name))

        def sems(name, n):
            return [sem(f"{name}{i}") for i in range(n)]

        bank = [ctx.enter_context(nc.psum_tensor(f"bank{i}", [128, 512], F32)) for i in range(8)]

        w_raw = sb("w_raw", [128, NC + 1, COLS])
        w_half = w_raw[:, :, :].bitcast(F16).rearrange("p c (s n) -> p c s n", s=2)
        spare = w_raw[:, NC, :]
        gate_a = [spare[:, 512 * i:512 * i + 512].rearrange("p (h n) -> p h n", h=4) for i in range(2)]
        gate_b = spare[:, 1024:1536].rearrange("p (h n) -> p h n", h=4)
        k_tail = spare[:, 1536:2048].rearrange("p (h n) -> p h n", h=4)
        post_w = spare[:, 2048:3072]
        w_o = sb("w_o", [128, NC, D])
        x_in = sb("x_in", [128, D])
        shared = sb("shared", [128, 1024])
        squares = shared[:, :].rearrange("p (h n) -> p h n", n=128)
        soft = squares
        x_half = shared[:, :].bitcast(F16).rearrange("p (s n) -> p s n", s=2)
        rot_in = shared[:, 0:512].rearrange("p (h n) -> p h n", h=8)
        rot_sw = shared[:, 512:1024].rearrange("p (h n) -> p h n", h=8)
        xt_half = sb("xt_half", [128, 2, NC, TOK], F16)
        conv_in = sb("conv_in", [128, 4, 3 + TOK])
        halo = sb("halo", [128, 12, 3])
        tanh_z = sb("tanh_z", [128, 512])
        tanh_c = sb("tanh_c", [128, 512])
        qkv = sb("qkv", [128, 12, TOK])
        q_rot = sb("q_rot", [128, 512])
        q_t = q_rot[:, :].rearrange("p (c n) -> p c n", c=4)
        k_raw = sb("k_raw", [128, 2, 64])
        k_sw = sb("k_sw", [128, 2, 64])
        k_rot = sb("k_rot", [128, 2, 2, 64])
        k_win = sb("k_win", [128, 2, 3 * CHUNK])
        v_tok = [sb(f"v_tok{i}", [128, 128]) for i in range(2)]
        v_win = sb("v_win", [128, 128])
        rot_tab = sb("rot_tab", [128, 128])
        decay = sb("decay", [128, 4, 128])
        mt = sb("mt", [128, 4, 128])
        cw = sb("cw", [128, 4, 128])
        inv_t = sb("inv_t", [128, 4, 128])
        inv_u = sb("inv_u", [128, 4, 128])
        prod = sb("prod", [128, 4, 128])
        unread = prod[:, :, :].rearrange("p h n -> p (h n)").bitcast(mybir.dt.bfloat16)
        rhs = sb("rhs", [128, 4, 128])
        state = sb("state", [128, 4, 128])
        out_b = sb("out_b", [128, 4, 128])
        y_out = sb("y_out", [128, D])
        masks = sb("masks", [128, LEVELS + 1, 128], F16)
        ident16 = masks[:, LEVELS, :]
        c32 = sb("c32", [128, 3, 128])
        ident, upper, neg = c32[:, 0, :], c32[:, 1, :], c32[:, 2, :]
        rows = x_in[0:57, 0:128]
        cols = sb("cols", [128, 57])
        conv_taps = cols[:, 0:48]
        small = sb("small", [128, 200])

        def cut(at, n):
            return small[:, at:at + n]

        unscale, half_unscale = cut(0, 1), cut(1, 1)
        neg_a, dt_bias, sinks8 = cut(2, 4), cut(6, 4), cut(10, 8)
        row_scale = cut(18, 8)
        w_max, w_amax, w_pow2, w_scale = cut(26, 8), cut(34, 2), cut(36, 1), cut(37, 1)
        power = cut(38, 16)
        g_cols = cut(54, 12)
        exp_cols = cut(66, 12)
        norms, key_inv, key_c, key_nc, key_norm = cut(78, 8), cut(86, 4), cut(90, 4), cut(94, 4), cut(98, 4)
        ab = cut(102, 8)
        soft_arg, soft_exp, beta_tanh, beta = cut(110, 4), cut(114, 4), cut(118, 4), cut(122, 4)
        g_tok = cut(126, 4)
        gtmp = [cut(130 + 4 * i, 4) for i in range(4)]
        row_max, sink_arg, row_sum = cut(146, 8), cut(154, 8), cut(162, 8)
        o_sq, o_arg, o_f = cut(170, 4), cut(174, 4), cut(178, 4)
        x_sq, x_arg, x_rs = cut(182, 1), cut(183, 1), cut(184, 1)
        y_sq, y_arg, y_rs = cut(185, 2), cut(187, 1), cut(188, 1)
        eps_sum, root_scale = cut(189, 1), cut(190, 1)

        const_loaded, x_loaded, rot_loaded, res_loaded, stored, wo_loaded, pw_loaded = (
            sem(n) for n in ("const_loaded", "x_loaded", "rot_loaded", "res_loaded",
                             "stored", "wo_loaded", "pw_loaded"))
        w_loaded = sems("w_loaded", NC)
        w_max_ready, w_amax_ready, w_scale_ready, w_hi_ready, w_lo_ready, wo_ready, cols_t, set_up = (
            sem(n) for n in ("w_max_ready", "w_amax_ready", "w_scale_ready", "w_hi_ready", "w_lo_ready",
                             "wo_ready", "cols_t", "set_up"))
        setup_link, neg_a_exp, pool_set, post_w_ready = (
            sem(n) for n in ("setup_link", "neg_a_exp", "pool_set", "post_w_ready"))
        x_sq_ready, x_rs_ready, xh_ready, xl_ready, x_turned, xt_ready = (
            sem(n) for n in ("x_sq_ready", "x_rs_ready", "xh_ready", "xl_ready", "x_turned", "xt_ready"))
        fill_ready = sems("fill_ready", 7)
        tanh_za_ready, tanh_zb_ready, gate_a_ready, gate_b_ready = (
            sem(n) for n in ("tanh_za_ready", "tanh_zb_ready", "gate_a_ready", "gate_b_ready"))
        conv_in_ready, conv_ready, tanh_c_ready, qkv_ready = (
            sems(n, 3) for n in ("conv_in_ready", "conv_ready", "tanh_c_ready", "qkv_ready"))
        k_win_moved = sem("k_win_moved")
        halo_used, conv_link, rot_link, x_link, pool_link = sem("halo_used"), sem("conv_link"), sem("rot_link"), sem("x_link"), sem("pool_link")
        kv_raw_ready, k_rot_ready, q_raw_ready, q_rot_ready, ab_ready = (
            sem(n) for n in ("kv_raw_ready", "k_rot_ready", "q_raw_ready", "q_rot_ready", "ab_ready"))
        gate_link, soft_arg_ready, soft_exp_ready, g_ready = (
            sem(n) for n in ("gate_link", "soft_arg_ready", "soft_exp_ready", "g_ready"))
        g_col_t, g_row_t, g_cols_used, decay_arg_ready, decay_ready, exp_cols_ready = (
            sem(n) for n in ("g_col_t", "g_row_t", "g_cols_used", "decay_arg_ready", "decay_ready",
                             "exp_cols_ready"))
        gram_t, k_turned, v_turned, q_turned, sq_ready = (
            sem(n) for n in ("gram_t", "k_turned", "v_turned", "q_turned", "sq_ready"))
        norm_link, norms_ready, key_norm_ready, m_ready, at_ready, vn_ready, k_tail_ready = (
            sem(n) for n in ("norm_link", "norms_ready", "key_norm_ready", "m_ready", "at_ready",
                             "vn_ready", "k_tail_ready"))
        c_ready, p_turn, p_ready, tp_turn, up_turn, t_ready, u_ready = (
            {lv: Nth(s, hi - lo + 1, lv - lo) for lv in range(lo, hi + 1)} for s, lo, hi in (
                (sem("c_ready"), 0, 6), (sem("p_turn"), 0, 6), (sem("p_ready"), 1, 6),
                (sem("tp_turn"), 1, 5), (sem("up_turn"), 1, 6), (sem("t_ready"), 0, 5),
                (sem("u_ready"), 0, 6)))
        qr_turned, kr_turned, q_t_ready, k_win_ready, v_win_ready, scores_ready = (
            sem(n) for n in ("qr_turned", "kr_turned", "q_t_ready", "k_win_ready", "v_win_ready",
                             "scores_ready"))
        soft_link, no_chunk, sub_ready, exp_ready, rsum_ready, soft_ready, soft_turned, soft_t_ready, pv_ready, \
            out_b_ready = (sem(n) for n in ("soft_link", "no_chunk", "sub_ready", "exp_ready", "rsum_ready", "soft_ready",
                                            "soft_turned", "soft_t_ready", "pv_ready", "out_b_ready"))
        ks_ready, rhs_ready, w_mm_ready, w_ready, qs_ready, qs_used, ds_ready, aw_ready, state_ready, o_ready = (
            sem(n) for n in ("ks_ready", "rhs_ready", "w_mm_ready", "w_ready", "qs_ready", "qs_used",
                             "ds_ready", "aw_ready", "state_ready", "o_ready"))
        o_sq_ready, o_link, o_arg_ready, o_f_ready, on_ready, o_turned, out_a_ready = (
            sem(n) for n in ("o_sq_ready", "o_link", "o_arg_ready", "o_f_ready", "on_ready", "o_turned",
                             "out_a_ready"))
        y_ready, y_sq_ready, y_rs_ready, y_used, post_ready = (
            sem(n) for n in ("y_ready", "y_sq_ready", "y_rs_ready", "y_used", "post_ready"))
        fill_used = {FILL_ZA: gate_a_ready, FILL_V: conv_in_ready[2], FILL_KVB: kv_raw_ready,
                     FILL_QB: q_raw_ready, FILL_ZB: gate_b_ready, FILL_K: conv_in_ready[1],
                     FILL_Q: conv_in_ready[0]}

        block = ctx.enter_context(nc.Block())

        def bc(ap, n):
            return ap.unsqueeze(2).broadcast_to([128, ap.shape[1], n])

        def over_heads(ap, h):
            return ap.unsqueeze(1).broadcast_to([128, h, ap.shape[1]])

        def heads(b):
            return bank[b][:, :].rearrange("p (h n) -> p h n", h=4)

        def run_steps(eng, step):
            step(0, 0, False, True, True)
            step(1, 1, True, True, True)
            with eng.Fori(0, NT // 2 - 2) as i:
                step(i * 2 + 2, 0, True, True, True)
                step(i * 2 + 3, 1, True, True, True)
            step(NT - 2, 0, True, True, True)
            step(NT - 1, 1, True, True, False)
            step(NT, 0, True, False, False)

        @block.sync
        def _(sp):
            sp.dma_start(rows[0:48, :], conv_w[0].rearrange("k (b p) -> (k b) p", p=128)).then_inc(const_loaded, 16)
            sp.dma_start(rows[48:56, :], pre_norm_w[0].rearrange("(c p) -> c p", p=128)).then_inc(const_loaded, 16)
            sp.dma_start(rows[56:57, :], dn_out_norm_w).then_inc(const_loaded, 16)
            sp.dma_start(c32[:, :, :], const32).then_inc(const_loaded, 16)
            sp.dma_start(masks[:, :, :], const16).then_inc(const_loaded, 16)
            sp.dma_start(neg_a, dn_a_log.broadcast_to([128, DN_HEADS])).then_inc(const_loaded, 16)
            sp.dma_start(dt_bias, dn_dt_bias.broadcast_to([128, DN_HEADS])).then_inc(const_loaded, 16)
            with nc.allow_non_contiguous_dma(reason="eight values, once"):
                for half in range(2):
                    sp.dma_start(sinks8[:, 4 * half:4 * half + 4],
                                 sw_sinks[:, half::2].broadcast_to([128, 4])).then_inc(const_loaded, 16)
            for c in range(NC):
                r = slice(128 * c, 128 * c + 128)
                for at, lo, hi in ((COL_Q, 0, 2048), (COL_ZB, 2824, 3336), (COL_QB, 2056, 2824),
                                   (COL_KVB + 256, 2048, 2056)):
                    sp.dma_start(w_raw[:, c + 1, at:at + hi - lo], w_in[0, r, lo:hi]).then_inc(w_loaded[c], 16)
            for c in range(NC):
                sp.dma_start(w_o[:, c, :], w_out[0, 128 * c:128 * c + 128, :]).then_inc(wo_loaded, 16)
            sp.wait_ge(cols_t, 1)
            sp.dma_start(x_in[:, :], x[0, 0:TOK, :]).then_inc(x_loaded, 16)
            sp.wait_ge(w_hi_ready, NC)
            sp.wait_ge(w_lo_ready, NC)
            sp.dma_start(post_w, post_norm_w.broadcast_to([128, D])).then_inc(pw_loaded, 16)

            def step(t, p, mix, proj, prep):
                m = t - 1
                if prep:
                    done(sp, xl_ready, t)
                    sp.dma_start(x_in[:, :], x[0, bass.ds((t + 1) * TOK, TOK), :]).then_inc(x_loaded, 16)
                if proj:
                    done(sp, q_rot_ready, m)
                    sp.dma_start(rot_tab[:, :], rotary[bass.ds(t * TOK, TOK), :]).then_inc(rot_loaded, 16)
                if mix:
                    if not (isinstance(m, int) and m == 0):
                        sp.wait_ge(stored, m * 16)
                    sp.dma_start(y_out[:, :], x[0, bass.ds(m * TOK, TOK), :]).then_inc(res_loaded, 16)
                    done(sp, post_ready, m)
                    sp.dma_start(out[0, bass.ds(m * TOK, TOK), :], y_out[:, :]).then_inc(stored, 16)

            run_steps(sp, step)
            sp.wait_ge(stored, NT * 16)

        @block.tensor
        def _(pe):
            mm = nc.tensor.matmul

            pe.wait_ge(const_loaded, 9 * 16)
            nc.tensor.transpose(bank[2][:, 0:57], rows, ident[0:57, 0:57]).then_inc(cols_t, 1)
            pe.wait_ge(set_up, 1)
            pe.wait_ge(pool_set, 1)

            def turn_x(n):
                done(pe, xh_ready, n)
                done(pe, w_ready, n - 2)
                done(pe, o_ready, n - 2)
                for s in range(2):
                    if s:
                        done(pe, xl_ready, n)
                    dst = bank[6 + s][:, :].bitcast(F16).rearrange("p (c n) -> p c n", c=NC)
                    for c in range(NC):
                        last = nc.tensor.transpose(dst[:, c, :], x_half[:, s, 128 * c:128 * c + 128], ident16)
                last.then_inc(x_turned, 1)

            def step(t, p, mix, proj, prep):
                m = t - 1
                queue = iter(PIECES)

                def fill(n):
                    if not proj:
                        return
                    for _ in range(n):
                        f, b = next(queue)
                        dst = bank[(p + f) % 2]
                        if (f, b) == (0, 0):
                            done(pe, xt_ready, t)
                        if b == 0:
                            done(pe, fill_used[(f - 2) % 7], t if f >= 2 else m)
                        if f in FILL_COL:
                            col = FILL_COL[f] + 128 * b
                            for c in range(NC):
                                for ws, xs in ((0, 0), (0, 1), (1, 0)):
                                    last = mm(dst[:, 128 * b:128 * b + 128], w_half[:, c, ws, col:col + 128],
                                              xt_half[:, xs, c, :], start=(c == 0 and ws + xs == 0),
                                              stop=(c == NC - 1 and ws == 1))
                        else:
                            col, n_col, per = (COL_QB, 512, NC // 4) if f == FILL_QB else (COL_KVB, KV, NC // 2)
                            for c in range(per * b, per * b + per):
                                for xs, ws in ((0, 0), (0, 1), (1, 0)):
                                    last = mm(dst[:, 0:n_col], xt_half[:, xs, c, :],
                                              w_half[:, c, ws, col:col + n_col], start=(c == 0 and ws + xs == 0),
                                              stop=(c == NC - 1 and xs == 1))
                        if (f, b + 1) not in PIECES:
                            last.then_inc(fill_ready[f], 1)

                def per_head(b, lhs, right, event=None, start=True, stop=True):
                    for h in range(4):
                        last = mm(bank[b][:, 128 * h:128 * h + 128], lhs[:, h, :],
                                  right[:, h, :] if len(right.shape) == 3 else right, start=start, stop=stop)
                    last.then_inc(event.sem if isinstance(event, Nth) else event, 1)

                def level_p(lv):
                    done(pe, c_ready[lv], m)
                    if lv:
                        done(pe, t_ready[lv - 1], m)
                    per_head(2, cw, inv_t if lv else ident, p_turn[lv])

                def level_tu(lv):
                    done(pe, p_ready[lv], m)
                    done(pe, u_ready[lv - 1], m)
                    if lv < LEVELS - 1:
                        per_head(2, inv_u, prod, tp_turn[lv])
                    done(pe, at_ready, m)
                    per_head(3, prod, inv_u, up_turn[lv])

                q4, k4, v4 = qkv[:, 0:4, :], qkv[:, 4:8, :], qkv[:, 8:12, :]
                if not mix:
                    fill(len(PIECES))
                    if prep:
                        turn_x(t + 1)
                    return
                done(pe, g_ready, m)
                done(pe, y_used, m - 1)
                mm(bank[4][:, 0:4], upper, g_tok, start=True, stop=True).then_inc(g_col_t, 1)
                for h in range(4):
                    last = mm(bank[5][:, 128 * h:128 * h + 128], g_tok[:, h:h + 1].broadcast_to([128, 128]),
                              upper, start=True, stop=True)
                last.then_inc(g_row_t, 1)
                for g in range(3):
                    done(pe, qkv_ready[g], m)
                done(pe, state_ready, m - 1)
                per_head(2, k4, k4, gram_t)
                done(pe, out_a_ready, m - 1)
                per_head(3, k4, q4, gram_t)
                done(pe, xt_ready, t if proj else m)
                done(pe, w_ready, m - 1)
                done(pe, o_ready, m - 1)
                for h in range(4):
                    last = nc.tensor.transpose(heads(6)[:, h, :], k4[:, h, :], ident)
                last.then_inc(k_turned, 1)
                for h in range(4):
                    last = nc.tensor.transpose(heads(7)[:, h, :], v4[:, h, :], ident)
                last.then_inc(v_turned, 1)
                done(pe, g_cols_used, m)
                for h in range(4):
                    last = nc.tensor.transpose(heads(4)[:, h, :], q4[:, h, :], ident)
                last.then_inc(q_turned, 1)
                fill(2)
                done(pe, q_rot_ready, m)
                done(pe, decay_arg_ready, m)
                for c in range(4):
                    last = nc.tensor.transpose(heads(5)[:, c, :], q_rot[:, 128 * c:128 * c + 128], ident)
                last.then_inc(qr_turned, 1)
                done(pe, k_rot_ready, m)
                done(pe, sq_ready, m)
                for kv in range(2):
                    last = nc.tensor.transpose(heads(4)[:, kv, :], k_rot[:, kv, :, :].rearrange("p d n -> p (d n)"), ident)
                last.then_inc(kr_turned, 1)
                fill(4)
                done(pe, q_t_ready, m)
                done(pe, k_win_ready, m)
                level_p(0)
                fill(1)
                first = isinstance(m, int) and m == 0
                for half in range(2):
                    rows_ = slice(64 * half, 64 * half + 64)
                    for c in range(4):
                        for a in range(2):
                            k0 = CHUNK if first and a == 0 else 0
                            last = mm(bank[4 + half][64 * a:64 * a + 64, 128 * c + k0:128 * c + 128],
                                      q_t[rows_, c, 64 * a:64 * a + 64],
                                      k_win[rows_, c // 2, CHUNK * a + k0:CHUNK * a + 128], start=True, stop=True)
                last.then_inc(scores_ready, 1)
                fill(1)
                level_p(1)
                fill(1)
                level_tu(1)
                fill(1)
                level_p(2)
                fill(1)
                level_tu(2)
                done(pe, soft_ready, m)
                for hh in range(8):
                    last = nc.tensor.transpose(heads(4 + hh // 4)[:, hh % 4, :], soft[:, hh, :], ident)
                last.then_inc(soft_turned, 1)
                fill(1)
                level_p(3)
                fill(1)
                done(pe, soft_t_ready, m)
                done(pe, v_win_ready, m)
                done(pe, k_tail_ready, m)
                for half in range(2):
                    for kv in range(2):
                        for a, v in enumerate((v_win, v_tok[1 - p])):
                            hh = 4 * half + 2 * kv
                            last = mm(heads(6)[64 * half:64 * half + 64, 2 * kv:2 * kv + 2, 64 * a:64 * a + 64],
                                      v[:, 64 * kv:64 * kv + 64], soft[:, hh:hh + 2, 64 * a:64 * a + 64],
                                      start=True, stop=True)
                last.then_inc(pv_ready, 1)
                level_tu(3)
                fill(1)
                level_p(4)
                fill(1)
                level_tu(4)
                fill(1)
                level_p(5)
                fill(1)
                level_tu(5)
                fill(1)
                done(pe, state_ready, m - 1)
                done(pe, vn_ready, m)
                per_head(7, k4, state, ks_ready)
                level_p(6)
                fill(1)
                level_tu(6)
                fill(1)
                done(pe, rhs_ready, m)
                done(pe, u_ready[LEVELS - 1], m)
                done(pe, out_b_ready, m)
                per_head(6, inv_u, rhs, w_mm_ready)
                per_head(3, q4, state, qs_ready)
                fill(2)
                done(pe, w_ready, m)
                per_head(2, k_tail, cw, ds_ready)
                per_head(7, decay, cw, aw_ready)
                fill(2)

                def project_out(chunks, src, begin, event=None):
                    for i, c in enumerate(chunks):
                        for n in range(2):
                            last = mm(bank[4 + n][:, :], src[:, i, :], w_o[:, c, 512 * n:512 * n + 512],
                                      start=(begin and i == 0), stop=(not begin and i == len(chunks) - 1))
                    if event is not None:
                        last.then_inc(event, 1)

                project_out(range(4, 8), out_b, True)
                done(pe, on_ready, m)
                done(pe, qs_used, m)
                for h in range(4):
                    last = nc.tensor.transpose(heads(3)[:, h, :], mt[:, h, :], ident)
                last.then_inc(o_turned, 1)
                fill(2)
                if prep:
                    turn_x(t + 1)
                done(pe, out_a_ready, m)
                project_out(range(0, 4), inv_t, False, y_ready)

            turn_x(0)
            run_steps(pe, step)

        @block.scalar
        def _(act):
            f = nc.scalar.activation
            act.wait_ge(const_loaded, 9 * 16)
            f(neg_a, neg_a, ACT.Exp).then_inc(neg_a_exp, 1)
            act.wait_ge(w_scale_ready, 1)
            for c in range(NC):
                act.wait_ge(w_loaded[c], 64)
                if c:
                    act.wait_ge(w_lo_ready, c)
                f(w_half[:, c, 0, :], w_raw[:, c + 1, :], ACT.Identity, scale=row_scale[:, c:c + 1]).then_inc(w_hi_ready, 1)
            act.wait_ge(wo_loaded, 16 * NC)
            for c in range(4):
                last = f(w_o[:, c, :], w_o[:, c, :], ACT.Identity, scale=cols[:, 56:57])
            last.then_inc(wo_ready, 1)

            def normalise(n):
                act.wait_ge(x_loaded, (n + 1) * 16)
                f(x_half[:, 0, :], x_in[:, :], ACT.Square, accum_out=x_sq).then_inc(x_sq_ready, 1)
                done(act, x_rs_ready, n)
                f(x_half[:, 0, :], x_in[:, :], ACT.Identity, scale=x_rs).then_inc(xh_ready, 1)

            def conv_fill(t, p, fl):
                g = GROUP[fl]
                prev = {2: 0, 1: 2, 0: 1}[g]
                done(act, fill_ready[fl], t)
                done(act, conv_ready[prev], t - 1 if g == 2 else t)
                done(act, conv_in_ready[g], t - 1)
                f(conv_in[:, :, 0:3], halo[:, 4 * g:4 * g + 4, :], ACT.Copy)
                f(conv_in[:, :, 3:3 + TOK], heads((p + fl) % 2), ACT.Copy).then_inc(halo_used, 1)
                done(act, Nth(halo_used, 3, {2: 0, 1: 1, 0: 2}[g]), t)
                f(halo[:, 4 * g:4 * g + 4, :], heads((p + fl) % 2)[:, :, TOK - 3:TOK], ACT.Copy).then_inc(
                    conv_in_ready[g], 1)

            def conv_tanh(t, g):
                prev = {2: 0, 1: 2, 0: 1}[g]
                done(act, conv_ready[g], t)
                done(act, qkv_ready[prev], t - 1 if g == 2 else t)
                f(tanh_c[:, :], qkv[:, 4 * g:4 * g + 4, :].rearrange("p h n -> p (h n)"), ACT.Tanh,
                  scale=0.5).then_inc(tanh_c_ready[g], 1)

            def tanh_gate(t, p, fl):
                done(act, fill_ready[fl], t)
                if fl == FILL_ZA:
                    done(act, gate_b_ready, t - 1)
                else:
                    done(act, gate_a_ready, t)
                f(tanh_z[:, :], bank[(p + fl) % 2][:, :], ACT.Tanh, scale=half_unscale).then_inc(
                    tanh_za_ready if fl == FILL_ZA else tanh_zb_ready, 1)

            def small_fill(t, p, mix):
                done(act, fill_ready[FILL_KVB], t)
                done(act, k_rot_ready, t - 1)
                done(act, g_ready, t - 1)
                b = bank[(p + FILL_KVB) % 2]
                f(ab, b[:, 256:264], ACT.Identity, scale=unscale).then_inc(ab_ready, 1)
                f(k_raw[:, :, :].rearrange("p h n -> p (h n)"), b[:, 0:128], ACT.Identity, scale=unscale)
                done(act, pv_ready, t - 2)
                f(v_tok[p][:, :], b[:, 128:256], ACT.Identity, scale=unscale).then_inc(kv_raw_ready, 1)
                act.wait_ge(ab_ready, t + 1)
                f(beta_tanh, ab[:, 0:4], ACT.Tanh, scale=0.5)
                done(act, soft_arg_ready, t)
                f(soft_exp, soft_arg, ACT.Exp).then_inc(soft_exp_ready, 1)

            def step(t, p, mix, proj, prep):
                m = t - 1
                first = isinstance(m, int) and m == 0

                def copy_p(lv):
                    done(act, p_turn[lv], m)
                    f(prod[:, :, :], heads(2), ACT.Copy).then_inc(p_ready[lv].sem, 1)

                if mix:
                    done(act, pv_ready, m - 1)
                    done(act, kv_raw_ready, m)
                    if not first:
                        f(v_win[0:64, :], v_tok[p][64:128, :], ACT.Copy)
                    f(v_win[64:128, :], v_tok[1 - p][0:64, :], ACT.Copy).then_inc(v_win_ready, 1)
                    done(act, decay_arg_ready, m)
                    f(exp_cols, g_cols, ACT.Exp).then_inc(exp_cols_ready, 1)
                    f(decay[:, :, :], decay[:, :, :], ACT.Exp).then_inc(decay_ready, 1)
                    done(act, k_turned, m)
                    done(act, post_ready, m - 1)
                    f(squares[:, 0:4, :], heads(6), ACT.Square)
                    done(act, q_turned, m)
                    f(squares[:, 4:8, :], heads(4), ACT.Square).then_inc(sq_ready, 1)
                    done(act, qr_turned, m)
                    f(q_t[:, :, :], heads(5), ACT.Copy).then_inc(q_t_ready, 1)
                    done(act, kr_turned, m)
                    if not first:
                        done(act, scores_ready, m - 1)
                        done(act, k_win_ready, m - 1)
                        f(k_win[:, :, 0:64], k_win[:, :, 128:192], ACT.Copy).then_inc(k_win_moved, 1)
                        act.wait_ge(k_win_moved, m)
                    f(k_win[:, :, 64:192], heads(4)[:, 0:2, :], ACT.Copy).then_inc(k_win_ready, 1)
                if proj:
                    tanh_gate(t, p, FILL_ZA)
                if proj:
                    conv_fill(t, p, FILL_V)
                if mix:
                    done(act, sub_ready, m)
                    f(sink_arg, sink_arg, ACT.Exp, scale=DH_B ** -0.5)
                    f(soft[:, :, :], soft[:, :, :], ACT.Exp, scale=DH_B ** -0.5).then_inc(exp_ready, 1)
                    copy_p(1)
                if proj:
                    conv_tanh(t, 2)
                if mix:
                    copy_p(2)
                if proj:
                    small_fill(t, p, mix)
                if mix:
                    copy_p(3)
                    done(act, soft_turned, m)
                    f(soft[:, 0:4, :], heads(4), ACT.Copy)
                    f(soft[:, 4:8, :], heads(5), ACT.Copy).then_inc(soft_t_ready, 1)
                    copy_p(4)
                if proj:
                    done(act, fill_ready[FILL_QB], t)
                    if mix:
                        done(act, pv_ready, m)
                    f(shared[:, 0:512], bank[(p + FILL_QB) % 2][:, :], ACT.Identity, scale=unscale).then_inc(
                        q_raw_ready, 1)
                if mix:
                    copy_p(5)
                if proj:
                    tanh_gate(t, p, FILL_ZB)
                if mix:
                    copy_p(6)
                if proj:
                    conv_fill(t, p, FILL_K)
                if prep:
                    done(act, q_rot_ready, t)
                    normalise(t + 1)
                if mix:
                    done(act, o_ready, m)
                    for h in range(4):
                        last = f(prod[:, h, :], mt[:, h, :], ACT.Square, accum_out=o_sq[:, h:h + 1])
                    last.then_inc(o_sq_ready, 1)
                if proj:
                    conv_tanh(t, 1)
                    conv_fill(t, p, FILL_Q)
                    conv_tanh(t, 0)
                if mix:
                    done(act, y_ready, m)
                    for n in range(2):
                        last = f(unread[:, 512 * n:512 * n + 512], bank[4 + n][:, :], ACT.Square,
                                 accum_out=y_sq[:, n:n + 1])
                    last.then_inc(y_sq_ready, 1)

            normalise(0)
            run_steps(act, step)

        @block.vector
        def _(dve):
            v = nc.vector
            dve.wait_ge(cols_t, 1)
            v.tensor_copy(cols[:, :], bank[2][:, 0:57]).then_inc(setup_link, 1)
            v.memset(halo[:, :, :], 0.0)
            v.memset(state[:, :, :], 0.0)
            v.memset(v_win[:, :], 0.0)
            dve.wait_ge(neg_a_exp, 1)
            v.tensor_scalar(neg_a, neg_a, -1.0, None, ALU.mult)
            v.tensor_scalar(sinks8, sinks8, DH_B ** 0.5, None, ALU.mult)
            for c in range(NC):
                dve.wait_ge(w_loaded[c], 64)
                last = v.tensor_reduce(w_max[:, c:c + 1], w_raw[:, c + 1, :], AX_X, ALU.max,
                                       apply_absolute_value=True)
            last.then_inc(setup_link, 1)
            dve.wait_ge(setup_link, 2)
            v.tensor_tensor(w_max, w_max, cols[:, 48:56], ALU.mult).then_inc(setup_link, 1)
            dve.wait_ge(setup_link, 3)
            v.tensor_reduce(w_amax[:, 0:1], w_max, AX_X, ALU.max, apply_absolute_value=True).then_inc(w_max_ready, 1)
            dve.wait_ge(w_amax_ready, 1)
            v.tensor_scalar(w_amax[:, 0:1], w_amax[:, 1:2], 1e-30, None, ALU.max).then_inc(setup_link, 1)
            dve.wait_ge(setup_link, 4)
            v.tensor_single_scalar(w_pow2.bitcast(I32), w_amax[:, 0:1].bitcast(I32), 0x7F800000,
                                   ALU.bitwise_and).then_inc(setup_link, 1)
            dve.wait_ge(setup_link, 5)
            v.reciprocal(w_scale, w_pow2).then_inc(setup_link, 1)
            dve.wait_ge(setup_link, 6)
            v.tensor_scalar(row_scale, cols[:, 48:56], w_scale, 2.0 ** 14, ALU.mult, ALU.mult).then_inc(w_scale_ready, 1)
            v.tensor_scalar(unscale, w_pow2, 2.0 ** -14 / X_SCALE, None, ALU.mult)
            v.tensor_scalar(half_unscale, w_pow2, 2.0 ** -15 / X_SCALE, None, ALU.mult).then_inc(setup_link, 1)
            dve.wait_ge(setup_link, 7)
            v.tensor_scalar(conv_taps, conv_taps, unscale, None, ALU.mult)
            for c in range(NC):
                dve.wait_ge(w_hi_ready, c + 1)
                if c == 0:
                    dve.wait_ge(w_scale_ready, 1)
                v.scalar_tensor_tensor(w_half[:, c, 1, :], w_raw[:, c + 1, :], row_scale[:, c:c + 1],
                                       w_half[:, c, 0, :], ALU.mult, ALU.subtract).then_inc(w_lo_ready, 1)
            dve.wait_ge(w_lo_ready, NC)
            v.memset(row_max, 0.0).then_inc(set_up, 1)
            dve.wait_ge(wo_ready, 1)
            dve.wait_ge(set_up, 1)

            def low_half(n):
                done(dve, xh_ready, n)
                v.scalar_tensor_tensor(x_half[:, 1, :], x_in[:, :], x_rs, x_half[:, 0, :], ALU.mult,
                                       ALU.subtract).then_inc(xl_ready, 1)

            def copy_xt(n, last_fill):
                done(dve, x_turned, n)
                if last_fill:
                    done(dve, fill_ready[FILL_Q], n - 1)
                for s in range(2):
                    last = v.tensor_copy(xt_half[:, s, :, :].rearrange("p c n -> p (c n)"),
                                         bank[6 + s][:, :].bitcast(F16))
                last.then_inc(xt_ready, 1)

            def convolve(t, fl, after):
                g = GROUP[fl]
                done(dve, conv_in_ready[g], t)
                for s, tile in after:
                    done(dve, s, tile)
                for i in range(4):
                    if i:
                        dve.wait_ge(conv_link, t * 9 + 3 * {2: 0, 1: 1, 0: 2}[g] + i)
                    for b in range(4):
                        tap = conv_taps[:, 12 * i + 4 * g + b:12 * i + 4 * g + b + 1]
                        dst = qkv[:, 4 * g + b, :]
                        if i == 0:
                            last = v.tensor_scalar(dst, conv_in[:, b, 0:TOK], tap, None, ALU.mult)
                        else:
                            last = v.scalar_tensor_tensor(dst, conv_in[:, b, i:i + TOK], tap, dst, ALU.mult, ALU.add)
                    last.then_inc(conv_ready[g] if i == 3 else conv_link, 1)

            def silu(t, g):
                done(dve, tanh_c_ready[g], t)
                y = qkv[:, 4 * g:4 * g + 4, :].rearrange("p h n -> p (h n)")
                v.scalar_tensor_tensor(y, tanh_c[:, :], 1.0, y, ALU.add, ALU.mult).then_inc(qkv_ready[g], 1)

            def gate(t, p, fl):
                done(dve, tanh_za_ready if fl == FILL_ZA else tanh_zb_ready, t)
                dst = gate_a[p] if fl == FILL_ZA else gate_b
                v.scalar_tensor_tensor(dst, tanh_z[:, :].rearrange("p (h n) -> p h n", h=4), 1.0,
                                       heads((p + fl) % 2), ALU.add, ALU.mult).then_inc(
                    gate_a_ready if fl == FILL_ZA else gate_b_ready, 1)

            def gates(t):
                count = [0]

                def link(ins):
                    count[0] += 1
                    ins.then_inc(gate_link, 1)
                    dve.wait_ge(gate_link, t * GATE_LINKS + count[0])

                u, a, z, z2 = gtmp
                done(dve, ab_ready, t)
                link(v.tensor_tensor(u, ab[:, 4:8], dt_bias, ALU.add))
                v.scalar_tensor_tensor(soft_arg, u, -1.0, u, ALU.mult, ALU.min).then_inc(soft_arg_ready, 1)
                done(dve, soft_exp_ready, t)
                v.tensor_scalar(beta, beta_tanh, 1.0, 0.5, ALU.add, ALU.mult)
                link(v.tensor_scalar(a, soft_exp, 2.0, None, ALU.add))
                link(v.reciprocal(z2, a))
                link(v.tensor_tensor(z, soft_exp, z2, ALU.mult))
                link(v.tensor_tensor(z2, z, z, ALU.mult))
                link(v.tensor_scalar(a, z2, SERIES[7], None, ALU.mult))
                for n in (6, 5, 4, 3, 2, 1):
                    link(v.scalar_tensor_tensor(a, a, SERIES[n], z2, ALU.add, ALU.mult))
                link(v.tensor_scalar(a, a, SERIES[0], None, ALU.add))
                link(v.scalar_tensor_tensor(z, a, 2.0, z, ALU.mult, ALU.mult))
                link(v.scalar_tensor_tensor(a, u, 0.0, z, ALU.max, ALU.add))
                v.tensor_tensor(g_tok, a, neg_a, ALU.mult).then_inc(g_ready, 1)
                assert count[0] == GATE_LINKS

            def step(t, p, mix, proj, prep):
                m = t - 1
                first = isinstance(m, int) and m == 0

                def update(lv):
                    if lv < LEVELS - 1:
                        done(dve, tp_turn[lv], m)
                        v.tensor_tensor(inv_t[:, :, :], inv_t[:, :, :], heads(2), ALU.subtract).then_inc(t_ready[lv].sem, 1)
                    done(dve, up_turn[lv], m)
                    v.tensor_tensor(inv_u[:, :, :], inv_u[:, :, :], heads(3), ALU.subtract).then_inc(u_ready[lv].sem, 1)

                if mix:
                    done(dve, g_col_t, m)
                    v.tensor_copy(g_cols[:, 0:4], bank[4][:, 0:4]).then_inc(g_cols_used, 1)
                    done(dve, g_row_t, m)
                    done(dve, exp_cols_ready, m - 1)
                    v.tensor_copy(g_cols[:, 8:12], heads(5)[:, :, TOK - 1]).then_inc(norm_link, 1)
                    dve.wait_ge(norm_link, m * 4 + 1)
                    v.tensor_tensor(g_cols[:, 4:8], g_cols[:, 8:12], g_cols[:, 0:4], ALU.subtract)
                    done(dve, aw_ready, m - 1)
                    for h in range(4):
                        last = v.scalar_tensor_tensor(decay[:, h, :], heads(5)[:, h, :], g_cols[:, h:h + 1], neg,
                                                      ALU.subtract, ALU.add)
                    last.then_inc(decay_arg_ready, 1)
                    done(dve, sq_ready, m)
                    v.tensor_reduce(norms, squares[:, :, :], AX_X, ALU.add).then_inc(norm_link, 1)
                    dve.wait_ge(norm_link, m * 4 + 2)
                    v.tensor_scalar(norms, norms, 0.25, EPS, ALU.mult, ALU.add).then_inc(norms_ready, 1)
                    done(dve, norms_ready, m)
                    v.reciprocal(key_inv, norms[:, 0:4]).then_inc(norm_link, 1)
                    dve.wait_ge(norm_link, m * 4 + 3)
                    done(dve, g_ready, m)
                    v.scalar_tensor_tensor(key_c, key_inv, 0.25, beta, ALU.mult, ALU.mult).then_inc(norm_link, 1)
                    dve.wait_ge(norm_link, m * 4 + 4)
                    v.tensor_scalar(key_nc, key_c, -1.0, None, ALU.mult)
                    done(dve, gram_t, m * 2 + 1)
                    done(dve, decay_ready, m)
                    done(dve, o_turned, m - 1)
                    for h in range(4):
                        last = v.scalar_tensor_tensor(mt[:, h, :], heads(2)[:, h, :], key_c[:, h:h + 1],
                                                      decay[:, h, :], ALU.mult, ALU.mult)
                    last.then_inc(m_ready, 1)
                    done(dve, m_ready, m)
                    v.tensor_tensor(decay[:, :, :], heads(3), decay[:, :, :], ALU.mult).then_inc(at_ready, 1)
                    done(dve, k_turned, m)
                    done(dve, exp_cols_ready, m)
                    done(dve, ds_ready, m - 1)
                    v.tensor_tensor(k_tail, heads(6), bc(exp_cols[:, 4:8], 128), ALU.mult).then_inc(k_tail_ready, 1)
                    done(dve, v_turned, m)
                    done(dve, key_norm_ready, m)
                    done(dve, w_mm_ready, m - 1)
                    v.tensor_tensor(rhs[:, :, :], heads(7), bc(key_norm, 128), ALU.mult).then_inc(vn_ready, 1)
                if proj:
                    gate(t, p, FILL_ZA)
                if mix:
                    done(dve, c_ready[0], m)
                    v.tensor_tensor(inv_u[:, :, :], over_heads(ident, 4), cw[:, :, :], ALU.subtract).then_inc(u_ready[0].sem, 1)
                    done(dve, p_turn[0], m)
                    done(dve, y_ready, m - 1)
                    v.tensor_tensor(inv_t[:, :, :], over_heads(ident, 4), heads(2), ALU.subtract).then_inc(t_ready[0].sem, 1)
                if mix:
                    done(dve, scores_ready, m)
                    if first:
                        for b in (4, 5):
                            last = v.memset(heads(b)[0:64, :, 0:64], NEG)
                        last.then_inc(no_chunk, 1)
                        dve.wait_ge(no_chunk, 1)
                    for half in range(2):
                        last = v.tensor_reduce(row_max[:, 4 * half:4 * half + 4], heads(4 + half), AX_X, ALU.max)
                    last.then_inc(soft_link, 1)
                    dve.wait_ge(soft_link, m * 5 + 1)
                    v.tensor_tensor(row_max, row_max, sinks8, ALU.max).then_inc(soft_link, 1)
                    dve.wait_ge(soft_link, m * 5 + 2)
                    v.tensor_tensor(sink_arg, sinks8, row_max, ALU.subtract)
                    for half in range(2):
                        last = v.tensor_tensor(soft[:, 4 * half:4 * half + 4, :], heads(4 + half),
                                               bc(row_max[:, 4 * half:4 * half + 4], 128), ALU.subtract)
                    last.then_inc(sub_ready, 1)
                if proj:
                    convolve(t, FILL_V, [(v_turned, m)] if mix else [])
                if mix:
                    update(1)
                    done(dve, exp_ready, m)
                    v.tensor_reduce(row_sum, soft[:, :, :], AX_X, ALU.add).then_inc(soft_link, 1)
                    dve.wait_ge(soft_link, m * 5 + 3)
                    v.tensor_tensor(row_sum, row_sum, sink_arg, ALU.add).then_inc(soft_link, 1)
                    dve.wait_ge(soft_link, m * 5 + 4)
                    v.reciprocal(row_max, row_sum).then_inc(soft_link, 1)
                    dve.wait_ge(soft_link, m * 5 + 5)
                    v.tensor_scalar(row_sum, row_max, half_unscale, None, ALU.mult).then_inc(rsum_ready, 1)
                if proj:
                    silu(t, 2)
                if mix:
                    update(2)
                if proj:
                    gates(t)
                if mix:
                    update(3)
                    done(dve, pv_ready, m)
                    done(dve, y_ready, m - 1)
                    v.tensor_tensor(out_b[:, :, :], heads(6), gate_b, ALU.mult).then_inc(out_b_ready, 1)
                    update(4)
                    update(5)
                if proj:
                    gate(t, p, FILL_ZB)
                if mix:
                    done(dve, ks_ready, m)
                    for h in range(4):
                        last = v.scalar_tensor_tensor(rhs[:, h, :], heads(7)[:, h, :], exp_cols[:, h:h + 1],
                                                      rhs[:, h, :], ALU.mult, ALU.subtract)
                    last.then_inc(rhs_ready, 1)
                    update(6)
                    done(dve, w_mm_ready, m)
                    v.tensor_tensor(cw[:, :, :], heads(6), bc(key_nc, 128), ALU.mult).then_inc(w_ready, 1)
                    done(dve, qs_ready, m)
                    v.tensor_tensor(mt[:, :, :], heads(3), bc(exp_cols[:, 0:4], 128), ALU.mult).then_inc(qs_used, 1)
                if proj:
                    convolve(t, FILL_K, [(ks_ready, m)] if mix else [])
                if mix:
                    done(dve, ds_ready, m)
                    for h in range(4):
                        last = v.scalar_tensor_tensor(state[:, h, :], state[:, h, :], exp_cols[:, 8 + h:9 + h],
                                                      heads(2)[:, h, :], ALU.mult, ALU.add)
                    last.then_inc(state_ready, 1)
                    done(dve, aw_ready, m)
                    done(dve, qs_used, m)
                    v.tensor_tensor(mt[:, :, :], mt[:, :, :], heads(7), ALU.add).then_inc(o_ready, 1)
                if prep:
                    low_half(t + 1)
                if mix:
                    done(dve, o_sq_ready, m)
                    v.tensor_scalar(o_arg, o_sq, 1.0 / 128, None, ALU.mult).then_inc(o_link, 1)
                    done(dve, o_link, m)
                    v.scalar_tensor_tensor(o_arg, norms[:, 4:8], EPS * 4 * 128, o_arg, ALU.mult, ALU.add).then_inc(
                        o_arg_ready, 1)
                if proj:
                    silu(t, 1)
                    convolve(t, FILL_Q, [(qs_ready, m)] if mix else [])
                if mix:
                    done(dve, o_turned, m)
                    v.tensor_tensor(inv_t[:, :, :], heads(3), gate_a[1 - p], ALU.mult).then_inc(out_a_ready, 1)
                if proj:
                    silu(t, 0)
                if prep:
                    copy_xt(t + 1, True)
                if mix:
                    if first:
                        dve.wait_ge(pw_loaded, 16)
                        v.tensor_scalar(post_w, post_w, D ** 0.5, None, ALU.mult).then_inc(post_w_ready, 1)
                        dve.wait_ge(post_w_ready, 1)
                    done(dve, y_rs_ready, m)
                    for n in range(2):
                        last = v.scalar_tensor_tensor(shared[:, 512 * n:512 * n + 512], bank[4 + n][:, :], y_rs,
                                                      post_w[:, 512 * n:512 * n + 512], ALU.mult, ALU.mult)
                    last.then_inc(y_used, 1)

            low_half(0)
            copy_xt(0, False)
            run_steps(dve, step)

        @block.gpsimd
        def _(pool):
            g = nc.gpsimd
            g.memset(power[:, 0:8], -0.5)
            g.memset(eps_sum, D * EPS)
            g.memset(root_scale, X_SCALE * D ** 0.5)
            g.memset(power[:, 8:16], 0.5).then_inc(pool_set, 1)
            pool.wait_ge(w_max_ready, 1)
            g.partition_all_reduce(w_amax[:, 1:2], w_amax[:, 0:1], 128, RMAX).then_inc(w_amax_ready, 1)
            pool.wait_ge(pool_set, 1)

            def rotate(dst, src, swap, n):
                cos, sin = rot_tab[:, 0:64], rot_tab[:, 64:128]
                g.tensor_tensor(dst, src, over_heads(cos, n), ALU.mult)
                for h in range(2):
                    last = g.tensor_tensor(swap[:, :, 32 * h:32 * h + 32], src[:, :, 32 - 32 * h:64 - 32 * h],
                                           over_heads(sin[:, 32 * h:32 * h + 32], n), ALU.mult)
                return last

            def step(t, p, mix, proj, prep):
                m = t - 1

                def coupling(lv):
                    if lv:
                        done(pool, p_turn[lv - 1], m)
                    g.tensor_tensor(cw[:, :, :], mt[:, :, :], over_heads(masks[:, lv, :], 4), ALU.mult).then_inc(
                        c_ready[lv].sem, 1)

                if mix:
                    done(pool, norms_ready, m)
                    g.tensor_tensor(key_norm, norms[:, 0:4], power[:, 8:12], ALU.pow).then_inc(key_norm_ready, 1)
                    done(pool, m_ready, m)
                    done(pool, ds_ready, m - 1)
                    done(pool, aw_ready, m - 1)
                    coupling(0)
                    done(pool, u_ready[0], m)
                    coupling(1)
                    coupling(2)
                    done(pool, rsum_ready, m)
                    g.tensor_tensor(soft[:, :, :], soft[:, :, :], bc(row_sum, 128), ALU.mult).then_inc(soft_ready, 1)
                    coupling(3)
                if proj:
                    pool.wait_ge(rot_loaded, (t + 1) * 16)
                    done(pool, kv_raw_ready, t)
                    if mix:
                        done(pool, kr_turned, m)
                    rotate(k_rot[:, :, 0, :], k_raw[:, :, :], k_sw[:, :, :], 2).then_inc(rot_link, 1)
                    pool.wait_ge(rot_link, t * 2 + 1)
                    g.tensor_tensor(k_rot[:, :, 1, :], k_rot[:, :, 0, :], k_sw[:, :, :], ALU.add)
                    g.tensor_tensor(k_rot[:, :, 0, :], k_rot[:, :, 0, :], k_sw[:, :, :], ALU.add).then_inc(k_rot_ready, 1)
                if mix:
                    coupling(4)
                if proj:
                    done(pool, q_raw_ready, t)
                    if mix:
                        done(pool, scores_ready, m)
                    q8 = q_rot[:, :].rearrange("p (h n) -> p h n", h=8)
                    rotate(q8, rot_in, rot_sw, 8).then_inc(rot_link, 1)
                    pool.wait_ge(rot_link, t * 2 + 2)
                    g.tensor_tensor(q8, q8, rot_sw, ALU.add).then_inc(q_rot_ready, 1)
                if mix:
                    coupling(5)
                    coupling(6)
                if prep:
                    root_x(t + 1)
                if mix:
                    done(pool, o_arg_ready, m)
                    g.tensor_tensor(o_f, o_arg, power[:, 0:4], ALU.pow).then_inc(o_f_ready, 1)
                    done(pool, o_f_ready, m)
                    g.tensor_tensor(o_f, o_f, half_unscale.broadcast_to([128, 4]), ALU.mult).then_inc(pool_link, 1)
                    pool.wait_ge(pool_link, m * 3 + 1)
                    g.tensor_tensor(mt[:, :, :], mt[:, :, :], bc(o_f, 128), ALU.mult).then_inc(on_ready, 1)
                    done(pool, y_sq_ready, m)
                    g.tensor_tensor(y_arg, y_sq[:, 0:1], y_sq[:, 1:2], ALU.add).then_inc(pool_link, 1)
                    pool.wait_ge(pool_link, m * 3 + 2)
                    g.tensor_tensor(y_arg, y_arg, eps_sum, ALU.add).then_inc(pool_link, 1)
                    pool.wait_ge(pool_link, m * 3 + 3)
                    g.tensor_tensor(y_rs, y_arg, power[:, 0:1], ALU.pow).then_inc(y_rs_ready, 1)
                    done(pool, y_used, m)
                    pool.wait_ge(res_loaded, (m + 1) * 16)
                    g.tensor_tensor(y_out[:, :], y_out[:, :], shared[:, :], ALU.add).then_inc(post_ready, 1)

            def root_x(n):
                done(pool, x_sq_ready, n)
                g.tensor_tensor(x_arg, x_sq, eps_sum, ALU.add).then_inc(x_link, 1)
                done(pool, Nth(x_link, 2, 0), n)
                g.tensor_tensor(x_arg, x_arg, power[:, 0:1], ALU.pow).then_inc(x_link, 1)
                done(pool, Nth(x_link, 2, 1), n)
                g.tensor_tensor(x_rs, x_arg, root_scale, ALU.mult).then_inc(x_rs_ready, 1)

            root_x(0)
            run_steps(pool, step)


_INS = ["x", "pre_norm_w", "w_in", "conv_w", "dn_a_log", "dn_dt_bias", "dn_out_norm_w", "sw_sinks", "w_out",
        "post_norm_w"]


def _constants(seq):
    import numpy as np

    n = TOK
    at = np.arange(n)
    ident = np.eye(n, dtype=np.float32)
    upper = (at[:, None] <= at[None, :]).astype(np.float32)
    neg = np.where(at[:, None] <= at[None, :], 0.0, NEG).astype(np.float32)
    const32 = np.ascontiguousarray(np.stack([ident, upper, neg], 1))
    masks = []
    for lv in range(LEVELS):
        m = 2 ** lv
        col, row = at[:, None], at[None, :]
        masks.append((col // (2 * m) == row // (2 * m)) & (col // m % 2 == 0) & (row // m % 2 == 1))
    const16 = np.ascontiguousarray(np.stack(masks + [np.eye(n, dtype=bool)], 1).astype(np.float16))
    half = DH_B // 2
    freq = (np.float32(10000.0) ** (-np.arange(half, dtype=np.float32) * np.float32(2.0) / np.float32(DH_B)))
    ang = (np.arange(seq, dtype=np.float32)[:, None] * freq.astype(np.float32)[None, :]).astype(np.float64)
    rotary = np.concatenate([np.cos(ang), np.cos(ang), -np.sin(ang), np.sin(ang)], 1).astype(np.float32)
    return {"const32": const32, "const16": const16, "rotary": rotary}


def kernel(**inputs):
    import numpy as np
    import concourse.bacc as bacc
    from concourse.bass_utils import run_bass_kernel_spmd as run

    nc = bacc.Bacc("TRN2", target_bir_lowering=False, num_devices=1)
    data = {name: np.ascontiguousarray(inputs[name]) for name in _INS}
    data.update(_constants(inputs["x"].shape[1]))
    arrays, args = {}, []
    for name, a in data.items():
        arrays[f"in_{name}_dram"] = a
        args.append(nc.dram_tensor(f"in_{name}_dram", a.shape, mybir.dt.from_np(a.dtype), kind="ExternalInput").ap())
    args.append(nc.dram_tensor("out_0_dram", data["x"].shape, F32, kind="ExternalOutput").ap())
    build(nc, *args)
    r = run(nc, [arrays], core_ids=[0])
    return r.results[0]["out_0_dram"]
```

```python
from contextlib import ExitStack

import concourse.bass as bass
from concourse import mybir

ALU = mybir.AluOpType
ACT = mybir.ActivationFunctionType
AX_X = mybir.AxisListType.X
F32 = mybir.dt.float32
F16 = mybir.dt.float16
I32 = mybir.dt.int32
RMAX, RSUM = bass.bass_isa.ReduceOp.max, bass.bass_isa.ReduceOp.add

TOK = 128
CHUNK = 64
EPS = 1e-6
DN_HEADS = 4
DH_B = 64
LEVELS = 7
GATE_LINKS = 15
NEG = -1e30
MIX_TOP = 60000.0
X_SCALE = 2.0 ** 10
SERIES = [1.0 / (2 * n + 1) for n in range(8)]

COL_Q, COL_K, COL_V, COL_ZA, COL_ZB, COL_QB, COL_KVB = 0, 512, 1024, 1536, 2048, 2560, 3072
FILL_ZA, FILL_V, FILL_KVB, FILL_QB, FILL_K, FILL_ZB, FILL_Q = range(7)
FILL_COL = {FILL_ZA: COL_ZA, FILL_V: COL_V, FILL_ZB: COL_ZB, FILL_K: COL_K, FILL_Q: COL_Q}
PIECES = [(f, b) for f in range(7) for b in range({FILL_KVB: 2}.get(f, 4))]
GROUP = {FILL_Q: 0, FILL_K: 1, FILL_V: 2}


class Nth:

    def __init__(self, sem, per, at):
        self.sem, self.per, self.at = sem, per, at


def done(eng, event, tile):
    if isinstance(tile, int) and tile < 0:
        return
    if isinstance(event, Nth):
        eng.wait_ge(event.sem, tile * event.per + (event.at + 1))
    else:
        eng.wait_ge(event, tile + 1)


def build(nc, x, pre_norm_w, w_in, conv_w, dn_a_log, dn_dt_bias, dn_out_norm_w, sw_sinks, w_out,
          post_norm_w, const32, const16, rotary, out):
    _, SEQ, D = x.shape
    COLS = w_in.shape[2]
    NT = SEQ // TOK
    NC = D // 128
    KV = COLS - COL_KVB
    assert NT % 2 == 0 and COL_KVB + KV == COLS

    with ExitStack() as ctx:
        def sb(name, shape, dt=F32):
            return ctx.enter_context(nc.sbuf_tensor(name, shape, dt))

        def sem(name):
            return ctx.enter_context(nc.semaphore(name))

        def sems(name, n):
            return [sem(f"{name}{i}") for i in range(n)]

        bank = [ctx.enter_context(nc.psum_tensor(f"bank{i}", [128, 512], F32)) for i in range(8)]

        w_raw = sb("w_raw", [128, NC + 1, COLS])
        w_half = w_raw[:, :, :].bitcast(F16).rearrange("p c (s n) -> p c s n", s=2)
        spare = w_raw[:, NC, :]
        gate_a = [spare[:, 512 * i:512 * i + 512].rearrange("p (h n) -> p h n", h=4) for i in range(2)]
        gate_b = spare[:, 1024:1536].rearrange("p (h n) -> p h n", h=4)
        k_tail = spare[:, 1536:2048].rearrange("p (h n) -> p h n", h=4)
        post_w = spare[:, 2048:3072]
        w_o = sb("w_o", [128, NC, D])
        x_in = sb("x_in", [128, D])
        shared = sb("shared", [128, 1024])
        soft = shared[:, :].rearrange("p (h n) -> p h n", n=128)
        x_half = shared[:, :].bitcast(F16).rearrange("p (s n) -> p s n", s=2)
        rot_in = shared[:, 0:512].rearrange("p (h n) -> p h n", h=8)
        rot_sw = shared[:, 512:1024].rearrange("p (h n) -> p h n", h=8)
        xt_half = sb("xt_half", [128, 2, NC, TOK], F16)
        conv_in = sb("conv_in", [128, 4, 3 + TOK])
        halo = sb("halo", [128, 12, 3])
        tanh_z = sb("tanh_z", [128, 512])
        tanh_c = sb("tanh_c", [128, 512])
        qkv = sb("qkv", [128, 12, TOK])
        q_rot = sb("q_rot", [128, 512])
        q_t = q_rot[:, :].rearrange("p (c n) -> p c n", c=4)
        k_raw = sb("k_raw", [128, 2, 64])
        k_sw = sb("k_sw", [128, 2, 64])
        k_rot = sb("k_rot", [128, 2, 2, 64])
        k_win = sb("k_win", [128, 2, 3 * CHUNK])
        v_tok = [sb(f"v_tok{i}", [128, 128]) for i in range(2)]
        v_win = sb("v_win", [128, 128])
        rot_tab = sb("rot_tab", [128, 128])
        decay = sb("decay", [128, 4, 128])
        mt = sb("mt", [128, 4, 128])
        cw = sb("cw", [128, 4, 128])
        inv_t = sb("inv_t", [128, 4, 128])
        inv_u = sb("inv_u", [128, 4, 128])
        out_a_half = inv_t[:, :, :].rearrange("p h n -> p (h n)").bitcast(F16).rearrange(
            "p (s h n) -> p s h n", s=2, h=4)
        prod = sb("prod", [128, 4, 128])
        unread = prod[:, :, :].rearrange("p h n -> p (h n)").bitcast(mybir.dt.bfloat16)
        rhs = sb("rhs", [128, 4, 128])
        state = sb("state", [128, 4, 128])
        out_b_half = sb("out_b_half", [128, 2, 4, 128], F16)
        y_out = sb("y_out", [128, D])

        def w_out_half(c):
            slot = w_o[:, (c - 1) % NC, :] if c >= 0 else y_out[:, :]
            return slot.bitcast(F16).rearrange("p (s n) -> p s n", s=2)

        masks = sb("masks", [128, LEVELS, 128], F16)
        ident16 = masks[:, LEVELS - 1, :]
        c32 = sb("c32", [128, 3, 128])
        ident, upper, neg = c32[:, 0, :], c32[:, 1, :], c32[:, 2, :]
        rows = x_in[0:57, 0:128]
        cols = sb("cols", [128, 57])
        conv_taps = cols[:, 0:48]
        small = sb("small", [128, 200])

        def cut(at, n):
            return small[:, at:at + n]

        unscale, half_unscale = cut(0, 1), cut(1, 1)
        neg_a, dt_bias, sinks8 = cut(2, 4), cut(6, 4), cut(10, 8)
        row_scale = cut(18, 8)
        w_max, w_amax, w_pow2, w_scale = cut(26, 8), cut(34, 2), cut(36, 1), cut(37, 1)
        power = cut(38, 16)
        g_cols = cut(54, 12)
        exp_cols = cut(66, 12)
        norms, key_inv, key_c, key_nc, key_norm = cut(78, 8), cut(86, 4), cut(90, 4), cut(94, 4), cut(98, 4)
        ab = cut(102, 8)
        soft_arg, soft_exp, beta_tanh, beta = cut(110, 4), cut(114, 4), cut(118, 4), cut(122, 4)
        g_tok = cut(126, 4)
        gtmp = [cut(130 + 4 * i, 4) for i in range(4)]
        row_max, sink_arg, row_sum = cut(146, 8), cut(154, 8), cut(162, 8)
        o_sq, o_arg, o_f = cut(170, 4), cut(174, 4), cut(178, 4)
        x_sq, x_arg, x_rs = cut(182, 1), cut(183, 1), cut(184, 1)
        y_sq, y_arg, y_rs = cut(185, 2), cut(187, 1), cut(188, 1)
        eps_sum, root_scale = cut(189, 1), cut(190, 1)
        out_f, mix_f, mix_bound, eps_y = cut(191, 1), cut(192, 1), cut(193, 1), cut(194, 1)
        wo_amax, wo_pow2, wo_scale = cut(195, 2), cut(197, 1), cut(198, 2)
        wo_max, w_sq, w_sum, w_total = w_max, row_max, x_sq, wo_pow2

        const_loaded, x_loaded, rot_loaded, res_loaded, stored, wo_loaded, pw_loaded = (
            sem(n) for n in ("const_loaded", "x_loaded", "rot_loaded", "res_loaded",
                             "stored", "wo_loaded", "pw_loaded"))
        w_loaded = sems("w_loaded", NC)
        w_sq_link, w_sum_ready, w_total_ready = (sem(n) for n in ("w_sq_link", "w_sum_ready", "w_total_ready"))
        w_max_ready, w_amax_ready, w_scale_ready, w_hi_ready, w_lo_ready, wo_max_ready, wo_amax_ready, wo_scale_ready, wo_hi_ready, wo_lo_ready, wo_ready, cols_t = (
            sem(n) for n in ("w_max_ready", "w_amax_ready", "w_scale_ready", "w_hi_ready", "w_lo_ready",
                             "wo_max_ready", "wo_amax_ready", "wo_scale_ready", "wo_hi_ready", "wo_lo_ready",
                             "wo_ready", "cols_t"))
        setup_link, neg_a_exp, pool_set, post_w_ready = (
            sem(n) for n in ("setup_link", "neg_a_exp", "pool_set", "post_w_ready"))
        x_sq_ready, x_rs_ready, xh_ready, xl_ready, x_turned, xt_ready = (
            sem(n) for n in ("x_sq_ready", "x_rs_ready", "xh_ready", "xl_ready", "x_turned", "xt_ready"))
        fill_ready = sems("fill_ready", 7)
        tanh_za_ready, tanh_zb_ready, gate_a_ready, gate_b_ready = (
            sem(n) for n in ("tanh_za_ready", "tanh_zb_ready", "gate_a_ready", "gate_b_ready"))
        conv_in_ready, conv_ready, tanh_c_ready, qkv_ready = (
            sems(n, 3) for n in ("conv_in_ready", "conv_ready", "tanh_c_ready", "qkv_ready"))
        k_win_moved = sem("k_win_moved")
        halo_used, conv_link, rot_link, x_link, pool_link = sem("halo_used"), sem("conv_link"), sem("rot_link"), sem("x_link"), sem("pool_link")
        kv_raw_ready, k_rot_ready, q_raw_ready, q_rot_ready, ab_ready = (
            sem(n) for n in ("kv_raw_ready", "k_rot_ready", "q_raw_ready", "q_rot_ready", "ab_ready"))
        gate_link, soft_arg_ready, soft_exp_ready, g_ready = (
            sem(n) for n in ("gate_link", "soft_arg_ready", "soft_exp_ready", "g_ready"))
        g_col_t, g_row_t, g_cols_used, decay_arg_ready, decay_ready, exp_cols_ready = (
            sem(n) for n in ("g_col_t", "g_row_t", "g_cols_used", "decay_arg_ready", "decay_ready",
                             "exp_cols_ready"))
        gram_t, k_turned, v_turned, q_turned, sq_ready = (
            sem(n) for n in ("gram_t", "k_turned", "v_turned", "q_turned", "sq_ready"))
        norm_link, k_norms_ready, norms_ready, key_norm_ready, m_ready, at_ready, vn_ready, k_tail_ready = (
            sem(n) for n in ("norm_link", "k_norms_ready", "norms_ready", "key_norm_ready", "m_ready", "at_ready",
                             "vn_ready", "k_tail_ready"))
        p_turn, p_ready, tp_turn, t_turned, t_ready, u_ready = (
            {lv: Nth(s, hi - lo + 1, lv - lo) for lv in range(lo, hi + 1)} for s, lo, hi in (
                (sem("p_turn"), 1, 6), (sem("p_ready"), 1, 6),
                (sem("tp_turn"), 1, 5), (sem("t_turned"), 1, 5), (sem("t_ready"), 1, 5),
                (sem("u_ready"), 1, 5)))
        c0_ready, u0_ready, u0_blank, u0_turned, t0_ready, p_clear = (
            sem(n) for n in ("c0_ready", "u0_ready", "u0_blank", "u0_turned", "t0_ready", "p_clear"))
        up_turn, inverse_ready, k_sq_ready, k_sq_used = (
            sem(n) for n in ("up_turn", "inverse_ready", "k_sq_ready", "k_sq_used"))
        qr_turned, kr_turned, q_t_ready, k_win_ready, v_win_ready, scores_ready = (
            sem(n) for n in ("qr_turned", "kr_turned", "q_t_ready", "k_win_ready", "v_win_ready",
                             "scores_ready"))
        soft_link, no_chunk, sub_ready, exp_ready, rsum_ready, soft_ready, soft_turned, soft_t_ready, pv_ready, \
            out_b_ready = (sem(n) for n in ("soft_link", "no_chunk", "sub_ready", "exp_ready", "rsum_ready", "soft_ready",
                                            "soft_turned", "soft_t_ready", "pv_ready", "out_b_ready"))
        ks_ready, rhs_ready, w_mm_ready, w_ready, qs_ready, qs_used, ds_ready, aw_ready, state_ready, o_ready = (
            sem(n) for n in ("ks_ready", "rhs_ready", "w_mm_ready", "w_ready", "qs_ready", "qs_used",
                             "ds_ready", "aw_ready", "state_ready", "o_ready"))
        o_sq_ready, o_link, o_arg_ready, o_f_ready, on_ready, o_turned, out_a_ready = (
            sem(n) for n in ("o_sq_ready", "o_link", "o_arg_ready", "o_f_ready", "on_ready", "o_turned",
                             "out_a_ready"))
        out_a_raw, out_a_high, out_b_raw, out_b_high = (
            sem(n) for n in ("out_a_raw", "out_a_high", "out_b_raw", "out_b_high"))
        y_ready, y_sq_ready, y_rs_ready, y_used, post_ready = (
            sem(n) for n in ("y_ready", "y_sq_ready", "y_rs_ready", "y_used", "post_ready"))
        fill_used = {FILL_ZA: gate_a_ready, FILL_V: conv_in_ready[2], FILL_KVB: kv_raw_ready,
                     FILL_QB: q_raw_ready, FILL_ZB: gate_b_ready, FILL_K: conv_in_ready[1],
                     FILL_Q: conv_in_ready[0]}

        block = ctx.enter_context(nc.Block())

        def bc(ap, n):
            return ap.unsqueeze(2).broadcast_to([128, ap.shape[1], n])

        def over_heads(ap, h):
            return ap.unsqueeze(1).broadcast_to([128, h, ap.shape[1]])

        def halves(ap, lv, which):
            a = " h" if len(ap.shape) == 3 else ""
            ap = ap.rearrange(f"p{a} (b s m) -> p{a} b s m", s=2, m=2 ** lv)
            return ap[:, :, :, which, :] if a else ap[:, :, which, :]

        def mask_halves(ap, lv, which, h=4):
            a = halves(ap, lv, which)
            return a.unsqueeze(1).broadcast_to([128, h, a.shape[1], a.shape[2]])

        def packed(b, at, lv):
            return bank[b][:, at:at + 256].rearrange("p (h b m) -> p h b m", h=4, m=2 ** lv)

        def heads(b):
            return bank[b][:, :].rearrange("p (h n) -> p h n", h=4)

        def run_steps(eng, step):
            step(0, 0, False, True, True)
            step(1, 1, True, True, True)
            with eng.Fori(0, NT // 2 - 2) as i:
                step(i * 2 + 2, 0, True, True, True)
                step(i * 2 + 3, 1, True, True, True)
            step(NT - 2, 0, True, True, True)
            step(NT - 1, 1, True, True, False)
            step(NT, 0, True, False, False)

        @block.sync
        def _(sp):
            sp.dma_start(rows[0:48, :], conv_w[0].rearrange("k (b p) -> (k b) p", p=128)).then_inc(const_loaded, 16)
            sp.dma_start(rows[48:56, :], pre_norm_w[0].rearrange("(c p) -> c p", p=128)).then_inc(const_loaded, 16)
            sp.dma_start(rows[56:57, :], dn_out_norm_w).then_inc(const_loaded, 16)
            sp.dma_start(c32[:, :, :], const32).then_inc(const_loaded, 16)
            sp.dma_start(masks[:, :, :], const16).then_inc(const_loaded, 16)
            sp.dma_start(neg_a, dn_a_log.broadcast_to([128, DN_HEADS])).then_inc(const_loaded, 16)
            sp.dma_start(dt_bias, dn_dt_bias.broadcast_to([128, DN_HEADS])).then_inc(const_loaded, 16)
            with nc.allow_non_contiguous_dma(reason="eight values, once"):
                for half in range(2):
                    sp.dma_start(sinks8[:, 4 * half:4 * half + 4],
                                 sw_sinks[:, half::2].broadcast_to([128, 4])).then_inc(const_loaded, 16)
            for c in range(NC):
                r = slice(128 * c, 128 * c + 128)
                for at, lo, hi in ((COL_Q, 0, 2048), (COL_ZB, 2824, 3336), (COL_QB, 2056, 2824),
                                   (COL_KVB + 256, 2048, 2056)):
                    sp.dma_start(w_raw[:, c + 1, at:at + hi - lo], w_in[0, r, lo:hi]).then_inc(w_loaded[c], 16)
                if c == 0:
                    sp.wait_ge(cols_t, 1)
                    sp.dma_start(x_in[:, :], x[0, 0:TOK, :]).then_inc(x_loaded, 16)
            for c in range(NC):
                sp.dma_start(w_o[:, c, :], w_out[0, 128 * c:128 * c + 128, :]).then_inc(wo_loaded, 16)
            sp.wait_ge(w_hi_ready, 2 * NC)
            sp.wait_ge(w_lo_ready, 2 * NC)
            sp.dma_start(post_w, post_norm_w.broadcast_to([128, D])).then_inc(pw_loaded, 16)

            def step(t, p, mix, proj, prep):
                m = t - 1
                if prep:
                    done(sp, xl_ready, t)
                    sp.dma_start(x_in[:, :], x[0, bass.ds((t + 1) * TOK, TOK), :]).then_inc(x_loaded, 16)
                if proj:
                    done(sp, q_rot_ready, m)
                    sp.dma_start(rot_tab[:, :], rotary[bass.ds(t * TOK, TOK), :]).then_inc(rot_loaded, 16)
                if mix:
                    if isinstance(m, int) and m == 0:
                        sp.wait_ge(wo_ready, 1)
                    else:
                        sp.wait_ge(stored, m * 16)
                    sp.dma_start(y_out[:, :], x[0, bass.ds(m * TOK, TOK), :]).then_inc(res_loaded, 16)
                    done(sp, post_ready, m)
                    sp.dma_start(out[0, bass.ds(m * TOK, TOK), :], y_out[:, :]).then_inc(stored, 16)

            run_steps(sp, step)
            sp.wait_ge(stored, NT * 16)

        @block.tensor
        def _(pe):
            mm = nc.tensor.matmul

            pe.wait_ge(const_loaded, 9 * 16)
            nc.tensor.transpose(bank[2][:, 0:57], rows, ident[0:57, 0:57]).then_inc(cols_t, 1)
            def turn_x(n):
                done(pe, xh_ready, n)
                done(pe, w_ready, n - 2)
                done(pe, o_ready, n - 2)
                for s in range(2):
                    if s:
                        done(pe, xl_ready, n)
                    dst = bank[6 + s][:, :].bitcast(F16).rearrange("p (c n) -> p c n", c=NC)
                    for c in range(NC):
                        last = nc.tensor.transpose(dst[:, c, :], x_half[:, s, 128 * c:128 * c + 128], ident16)
                last.then_inc(x_turned, 1)

            def step(t, p, mix, proj, prep):
                m = t - 1
                queue = iter(PIECES)

                def fill(n):
                    if not proj:
                        return
                    for _ in range(n):
                        f, b = next(queue)
                        dst = bank[(p + f) % 2]
                        if (f, b) == (0, 0):
                            done(pe, xt_ready, t)
                        if b == 0:
                            done(pe, fill_used[(f - 2) % 7], t if f >= 2 else m)
                        if f in FILL_COL:
                            col = FILL_COL[f] + 128 * b
                            for c in range(NC):
                                for ws, xs in ((0, 0), (0, 1), (1, 0)):
                                    last = mm(dst[:, 128 * b:128 * b + 128], w_half[:, c, ws, col:col + 128],
                                              xt_half[:, xs, c, :], start=(c == 0 and ws + xs == 0),
                                              stop=(c == NC - 1 and ws == 1))
                        else:
                            col, n_col, per = (COL_QB, 512, NC // 4) if f == FILL_QB else (COL_KVB, KV, NC // 2)
                            for c in range(per * b, per * b + per):
                                for xs, ws in ((0, 0), (0, 1), (1, 0)):
                                    last = mm(dst[:, 0:n_col], xt_half[:, xs, c, :],
                                              w_half[:, c, ws, col:col + n_col], start=(c == 0 and ws + xs == 0),
                                              stop=(c == NC - 1 and xs == 1))
                        if (f, b + 1) not in PIECES:
                            last.then_inc(fill_ready[f], 1)

                def per_head(b, lhs, right, event=None, start=True, stop=True):
                    for h in range(4):
                        last = mm(bank[b][:, 128 * h:128 * h + 128], lhs[:, h, :],
                                  right[:, h, :] if len(right.shape) == 3 else right, start=start, stop=stop)
                    last.then_inc(event.sem if isinstance(event, Nth) else event, 1)

                def half_heads(b, at, lhs, right, event, parts=128):
                    for h in range(4):
                        last = mm(bank[b][0:parts, at + 64 * h:at + 64 * h + 64], lhs[:, h, 0:parts],
                                  right[:, h, :, :], start=True, stop=True)
                    last.then_inc(event.sem if isinstance(event, Nth) else event, 1)

                def level_p(lv):
                    done(pe, t_ready[lv - 1] if lv > 1 else t0_ready, m)
                    if lv < LEVELS - 1:
                        half_heads(2, 0, mt, halves(inv_t[:, :, :], lv, 0), p_turn[lv])
                    else:
                        for h in range(4):
                            last = mm(bank[2][64:128, 64 * h:64 * h + 64], mt[:, h, 64:128], inv_t[:, h, 0:64],
                                      start=True, stop=True)
                        last.then_inc(p_turn[lv].sem, 1)
                    if lv == 1:
                        return
                    for h in range(4):
                        last = nc.tensor.transpose(heads(3)[:, h, :], inv_t[:, h, :], ident)
                    last.then_inc(t_turned[lv - 1].sem, 1)

                def level_t(lv):
                    done(pe, p_ready[lv], m)
                    if lv > 1:
                        done(pe, u_ready[lv - 1], m)
                    if lv < LEVELS - 1:
                        half_heads(2, 256, inv_u, halves(prod[:, :, :], lv, 0), tp_turn[lv])
                    else:
                        done(pe, p_clear, m)
                        half_heads(3, 0, prod, halves(inv_u[:, :, :], lv, 1), up_turn, 64)

                q4, k4, v4 = qkv[:, 0:4, :], qkv[:, 4:8, :], qkv[:, 8:12, :]
                if not mix:
                    fill(len(PIECES))
                    if prep:
                        turn_x(t + 1)
                    return
                done(pe, g_ready, m)
                done(pe, state_ready, m - 1)
                for h in range(4):
                    last = mm(bank[2][:, 128 * h:128 * h + 128], g_tok[:, h:h + 1].broadcast_to([128, 128]),
                              upper, start=True, stop=True)
                last.then_inc(g_row_t, 1)
                done(pe, out_a_ready, m - 1)
                mm(bank[3][:, 0:4], upper, g_tok, start=True, stop=True).then_inc(g_col_t, 1)
                done(pe, qkv_ready[1], m)
                done(pe, xt_ready, t if proj else m)
                done(pe, w_ready, m - 1)
                done(pe, o_ready, m - 1)
                for h in range(4):
                    last = nc.tensor.transpose(heads(6)[:, h, :], k4[:, h, :], ident)
                last.then_inc(k_turned, 1)
                done(pe, qkv_ready[2], m)
                for h in range(4):
                    last = nc.tensor.transpose(heads(7)[:, h, :], v4[:, h, :], ident)
                last.then_inc(v_turned, 1)
                fill(3)
                done(pe, y_used, m - 1)
                per_head(4, k4, k4, gram_t)
                done(pe, qkv_ready[0], m)
                per_head(5, k4, q4, gram_t)
                done(pe, g_cols_used, m)
                for h in range(4):
                    last = nc.tensor.transpose(heads(3)[:, h, :], q4[:, h, :], ident)
                last.then_inc(q_turned, 1)
                fill(2)
                done(pe, q_rot_ready, m)
                done(pe, decay_arg_ready, m)
                for c in range(4):
                    last = nc.tensor.transpose(heads(2)[:, c, :], q_rot[:, 128 * c:128 * c + 128], ident)
                last.then_inc(qr_turned, 1)
                done(pe, k_rot_ready, m)
                done(pe, sq_ready, m)
                for kv in range(2):
                    last = nc.tensor.transpose(heads(3)[:, kv, :], k_rot[:, kv, :, :].rearrange("p d n -> p (d n)"), ident)
                last.then_inc(kr_turned, 1)
                fill(2)
                done(pe, u0_ready, m)
                done(pe, u0_blank, m)
                done(pe, q_t_ready, m)
                for h in range(4):
                    last = nc.tensor.transpose(heads(2)[:, h, :], inv_u[:, h, :], ident)
                last.then_inc(u0_turned, 1)
                done(pe, k_win_ready, m)
                done(pe, at_ready, m)
                fill(1)
                first = isinstance(m, int) and m == 0
                for half in range(2):
                    rows_ = slice(64 * half, 64 * half + 64)
                    for c in range(4):
                        for a in range(2):
                            k0 = CHUNK if first and a == 0 else 0
                            last = mm(bank[4 + half][64 * a:64 * a + 64, 128 * c + k0:128 * c + 128],
                                      q_t[rows_, c, 64 * a:64 * a + 64],
                                      k_win[rows_, c // 2, CHUNK * a + k0:CHUNK * a + 128], start=True, stop=True)
                last.then_inc(scores_ready, 1)
                fill(1)
                level_p(1)
                fill(1)
                level_t(1)
                fill(1)
                level_p(2)
                done(pe, state_ready, m - 1)
                done(pe, vn_ready, m)
                per_head(7, k4, state, ks_ready)
                fill(1)
                level_t(2)
                fill(1)
                level_p(3)
                done(pe, soft_ready, m)
                for hh in range(8):
                    last = nc.tensor.transpose(heads(4 + hh // 4)[:, hh % 4, :], soft[:, hh, :], ident)
                last.then_inc(soft_turned, 1)
                fill(1)
                level_t(3)
                fill(1)
                done(pe, soft_t_ready, m)
                done(pe, v_win_ready, m)
                done(pe, k_tail_ready, m)
                for half in range(2):
                    for kv in range(2):
                        for a, v in enumerate((v_win, v_tok[1 - p])):
                            hh = 4 * half + 2 * kv
                            last = mm(heads(6)[64 * half:64 * half + 64, 2 * kv:2 * kv + 2, 64 * a:64 * a + 64],
                                      v[:, 64 * kv:64 * kv + 64], soft[:, hh:hh + 2, 64 * a:64 * a + 64],
                                      start=True, stop=True)
                last.then_inc(pv_ready, 1)
                level_p(4)
                fill(1)
                level_t(4)
                fill(1)
                level_p(5)
                fill(1)
                level_t(5)
                fill(1)
                level_p(6)
                fill(1)
                level_t(6)
                fill(1)
                done(pe, rhs_ready, m)
                done(pe, inverse_ready, m)
                done(pe, out_b_ready, m)
                per_head(6, inv_u, rhs, w_mm_ready)
                per_head(3, q4, state, qs_ready)
                fill(1)
                done(pe, w_ready, m)
                per_head(2, k_tail, cw, ds_ready)
                per_head(7, decay, cw, aw_ready)
                fill(2)

                def project_out(chunks, src, begin, event=None):
                    for i, c in enumerate(chunks):
                        for xs, ws in ((0, 0), (0, 1), (1, 0)):
                            for n in range(2):
                                last = mm(bank[4 + n][:, :], src[:, xs, i, :],
                                          w_out_half(c)[:, ws, 512 * n:512 * n + 512],
                                          start=(begin and i == 0 and xs + ws == 0),
                                          stop=(not begin and i == len(chunks) - 1 and xs == 1))
                    if event is not None:
                        last.then_inc(event, 1)

                if first:
                    pe.wait_ge(wo_ready, 1)
                project_out(range(4, 8), out_b_half, True)
                done(pe, on_ready, m)
                done(pe, qs_used, m)
                for h in range(4):
                    last = nc.tensor.transpose(heads(3)[:, h, :], mt[:, h, :], ident)
                last.then_inc(o_turned, 1)
                fill(2)
                if prep:
                    turn_x(t + 1)
                done(pe, out_a_ready, m)
                project_out(range(0, 4), out_a_half, False, y_ready)

            turn_x(0)
            pe.wait_ge(w_lo_ready, 2 * NC)
            run_steps(pe, step)

        @block.scalar
        def _(act):
            f = nc.scalar.activation
            act.wait_ge(const_loaded, 9 * 16)
            f(neg_a, neg_a, ACT.Exp).then_inc(neg_a_exp, 1)
            def normalise(n):
                act.wait_ge(x_loaded, (n + 1) * 16)
                f(x_half[:, 0, :], x_in[:, :], ACT.Square, accum_out=x_sq).then_inc(x_sq_ready, 1)
                done(act, x_rs_ready, n)
                f(x_half[:, 0, :], x_in[:, :], ACT.Identity, scale=x_rs).then_inc(xh_ready, 1)

            def w_out_high(part):
                act.wait_ge(wo_scale_ready, 1)
                for c in (2 * part, 2 * part + 1):
                    if c:
                        act.wait_ge(wo_lo_ready, c)
                    f(w_out_half(c if c else -1)[:, 0, :], w_o[:, c, :], ACT.Identity,
                      scale=wo_scale[:, c // 4:c // 4 + 1]).then_inc(wo_hi_ready, 1)

            def conv_fill(t, p, fl):
                g = GROUP[fl]
                prev = {2: 0, 1: 2, 0: 1}[g]
                done(act, fill_ready[fl], t)
                done(act, conv_ready[prev], t - 1 if g == 2 else t)
                done(act, conv_in_ready[g], t - 1)
                f(conv_in[:, :, 0:3], halo[:, 4 * g:4 * g + 4, :], ACT.Copy)
                f(conv_in[:, :, 3:3 + TOK], heads((p + fl) % 2), ACT.Copy).then_inc(halo_used, 1)
                done(act, Nth(halo_used, 3, {2: 0, 1: 1, 0: 2}[g]), t)
                f(halo[:, 4 * g:4 * g + 4, :], heads((p + fl) % 2)[:, :, TOK - 3:TOK], ACT.Copy).then_inc(
                    conv_in_ready[g], 1)

            def conv_tanh(t, g):
                prev = {2: 0, 1: 2, 0: 1}[g]
                done(act, conv_ready[g], t)
                done(act, qkv_ready[prev], t - 1 if g == 2 else t)
                f(tanh_c[:, :], qkv[:, 4 * g:4 * g + 4, :].rearrange("p h n -> p (h n)"), ACT.Tanh,
                  scale=0.5).then_inc(tanh_c_ready[g], 1)

            def tanh_gate(t, p, fl):
                done(act, fill_ready[fl], t)
                if fl == FILL_ZA:
                    done(act, gate_b_ready, t - 1)
                else:
                    done(act, gate_a_ready, t)
                f(tanh_z[:, :], bank[(p + fl) % 2][:, :], ACT.Tanh, scale=half_unscale).then_inc(
                    tanh_za_ready if fl == FILL_ZA else tanh_zb_ready, 1)

            def small_fill(t, p):
                done(act, fill_ready[FILL_KVB], t)
                done(act, k_rot_ready, t - 1)
                done(act, g_ready, t - 1)
                b = bank[(p + FILL_KVB) % 2]
                f(ab, b[:, 256:264], ACT.Identity, scale=unscale).then_inc(ab_ready, 1)
                f(k_raw[:, :, :].rearrange("p h n -> p (h n)"), b[:, 0:128], ACT.Identity, scale=unscale)
                done(act, pv_ready, t - 2)
                f(v_tok[p][:, :], b[:, 128:256], ACT.Identity, scale=unscale).then_inc(kv_raw_ready, 1)
                act.wait_ge(ab_ready, t + 1)
                f(beta_tanh, ab[:, 0:4], ACT.Tanh, scale=0.5)

            def step(t, p, mix, proj, prep):
                m = t - 1
                first = isinstance(m, int) and m == 0

                def copy_u(lv):
                    done(act, t_turned[lv], m)
                    f(inv_u[:, :, :], heads(3), ACT.Copy).then_inc(u_ready[lv].sem, 1)

                if mix:
                    done(act, pv_ready, m - 1)
                    done(act, kv_raw_ready, m)
                    if not first:
                        f(v_win[0:64, :], v_tok[p][64:128, :], ACT.Copy)
                    f(v_win[64:128, :], v_tok[1 - p][0:64, :], ACT.Copy).then_inc(v_win_ready, 1)
                    done(act, k_turned, m)
                    done(act, y_sq_ready, m - 1)
                    f(prod[:, :, :], heads(6), ACT.Square).then_inc(k_sq_ready, 1)
                    done(act, decay_arg_ready, m)
                    f(exp_cols, g_cols, ACT.Exp).then_inc(exp_cols_ready, 1)
                    f(decay[:, :, :], decay[:, :, :], ACT.Exp).then_inc(decay_ready, 1)
                    done(act, q_turned, m)
                    done(act, ds_ready, m - 1)
                    f(k_tail, heads(3), ACT.Square).then_inc(sq_ready, 1)
                    done(act, qr_turned, m)
                    f(q_t[:, :, :], heads(2), ACT.Copy).then_inc(q_t_ready, 1)
                    done(act, kr_turned, m)
                    if not first:
                        done(act, scores_ready, m - 1)
                        done(act, k_win_ready, m - 1)
                        f(k_win[:, :, 0:64], k_win[:, :, 128:192], ACT.Copy).then_inc(k_win_moved, 1)
                        act.wait_ge(k_win_moved, m)
                    f(k_win[:, :, 64:192], heads(3)[:, 0:2, :], ACT.Copy).then_inc(k_win_ready, 1)
                    done(act, u0_turned, m)
                    f(inv_t[:, :, :], heads(2), ACT.Copy).then_inc(t0_ready, 1)
                if proj:
                    tanh_gate(t, p, FILL_ZA)
                    conv_fill(t, p, FILL_V)
                    if not mix:
                        w_out_high(0)
                if mix:
                    done(act, sub_ready, m)
                    f(sink_arg, sink_arg, ACT.Exp, scale=DH_B ** -0.5)
                    f(soft[:, :, :], soft[:, :, :], ACT.Exp, scale=DH_B ** -0.5).then_inc(exp_ready, 1)
                    copy_u(1)
                if proj:
                    small_fill(t, p)
                    if not mix:
                        w_out_high(1)
                if mix:
                    copy_u(2)
                    done(act, soft_turned, m)
                    f(soft[:, 0:4, :], heads(4), ACT.Copy)
                    f(soft[:, 4:8, :], heads(5), ACT.Copy).then_inc(soft_t_ready, 1)
                if proj:
                    done(act, soft_arg_ready, t)
                    f(soft_exp, soft_arg, ACT.Exp).then_inc(soft_exp_ready, 1)
                if mix:
                    copy_u(3)
                if proj:
                    done(act, fill_ready[FILL_QB], t)
                    if mix:
                        done(act, pv_ready, m)
                    f(shared[:, 0:512], bank[(p + FILL_QB) % 2][:, :], ACT.Identity, scale=unscale).then_inc(
                        q_raw_ready, 1)
                    conv_tanh(t, 2)
                if mix:
                    copy_u(4)
                if proj:
                    conv_fill(t, p, FILL_K)
                if mix:
                    copy_u(5)
                    done(act, out_b_raw, m)
                    f(out_b_half[:, 0, :, :], heads(6), ACT.Copy).then_inc(out_b_high, 1)
                if prep:
                    done(act, q_rot_ready, t)
                    normalise(t + 1)
                if proj:
                    tanh_gate(t, p, FILL_ZB)
                    if not mix:
                        w_out_high(2)
                if mix:
                    done(act, o_ready, m)
                    for h in range(4):
                        last = f(prod[:, h, :], mt[:, h, :], ACT.Square, accum_out=o_sq[:, h:h + 1])
                    last.then_inc(o_sq_ready, 1)
                if proj:
                    conv_tanh(t, 1)
                if mix:
                    done(act, out_a_raw, m)
                    f(out_a_half[:, 0, :, :], heads(3), ACT.Copy).then_inc(out_a_high, 1)
                if proj:
                    conv_fill(t, p, FILL_Q)
                    conv_tanh(t, 0)
                    if not mix:
                        w_out_high(3)
                if mix:
                    done(act, y_ready, m)
                    for n in range(2):
                        last = f(unread[:, 512 * n:512 * n + 512], bank[4 + n][:, :], ACT.Square,
                                 accum_out=y_sq[:, n:n + 1])
                    last.then_inc(y_sq_ready, 1)

            normalise(0)
            act.wait_ge(w_scale_ready, 1)
            for c in range(NC):
                act.wait_ge(w_loaded[c], 64)
                for part in range(2):
                    r = slice(COLS // 2 * part, COLS // 2 * part + COLS // 2)
                    if c and part == 0:
                        act.wait_ge(w_lo_ready, 2 * c - 1)
                    f(w_half[:, c, 0, r], w_raw[:, c + 1, r], ACT.Identity, scale=row_scale[:, c:c + 1]).then_inc(
                        w_hi_ready, 1)
            run_steps(act, step)

        @block.vector
        def _(dve):
            v = nc.vector
            dve.wait_ge(cols_t, 1)
            v.tensor_copy(cols[:, :], bank[2][:, 0:57]).then_inc(setup_link, 1)
            v.memset(halo[:, :, :], 0.0)
            v.memset(state[:, :, :], 0.0)
            v.memset(v_win[:, :], 0.0)
            dve.wait_ge(neg_a_exp, 1)
            v.tensor_scalar(neg_a, neg_a, -1.0, None, ALU.mult)
            v.tensor_scalar(sinks8, sinks8, DH_B ** 0.5, None, ALU.mult)
            def low_half(n):
                done(dve, xh_ready, n)
                v.scalar_tensor_tensor(x_half[:, 1, :], x_in[:, :], x_rs, x_half[:, 0, :], ALU.mult,
                                       ALU.subtract).then_inc(xl_ready, 1)

            def copy_xt(n, last_fill):
                done(dve, x_turned, n)
                if last_fill:
                    done(dve, fill_ready[FILL_Q], n - 1)
                for s in range(2):
                    last = v.tensor_copy(xt_half[:, s, :, :].rearrange("p c n -> p (c n)"),
                                         bank[6 + s][:, :].bitcast(F16))
                last.then_inc(xt_ready, 1)

            def w_out_low(part):
                for c in (2 * part, 2 * part + 1):
                    dve.wait_ge(wo_hi_ready, c + 1)
                    if c:
                        dve.wait_ge(wo_lo_ready, c)
                    dst = w_out_half(c if c else -1)
                    v.scalar_tensor_tensor(dst[:, 1, :], w_o[:, c, :], wo_scale[:, c // 4:c // 4 + 1], dst[:, 0, :],
                                           ALU.mult, ALU.subtract).then_inc(wo_lo_ready, 1)
                if c == NC - 1:
                    dve.wait_ge(wo_lo_ready, NC)
                    v.tensor_copy(w_out_half(0), w_out_half(-1)).then_inc(wo_ready, 1)

            def convolve(t, fl, taps=range(4), after=None, tile=0, between=iter(())):
                g = GROUP[fl]
                for i in taps:
                    if i == 0:
                        done(dve, conv_in_ready[g], t)
                        if after is not None:
                            done(dve, after, tile)
                    if i:
                        dve.wait_ge(conv_link, t * 9 + 3 * {2: 0, 1: 1, 0: 2}[g] + i)
                    for b in range(4):
                        tap = conv_taps[:, 12 * i + 4 * g + b:12 * i + 4 * g + b + 1]
                        dst = qkv[:, 4 * g + b, :]
                        if i == 0:
                            last = v.tensor_scalar(dst, conv_in[:, b, 0:TOK], tap, None, ALU.mult)
                        else:
                            last = v.scalar_tensor_tensor(dst, conv_in[:, b, i:i + TOK], tap, dst, ALU.mult, ALU.add)
                        if b == 3:
                            last.then_inc(conv_ready[g] if i == 3 else conv_link, 1)
                        next(between, None)

            def silu(t, g):
                done(dve, tanh_c_ready[g], t)
                y = qkv[:, 4 * g:4 * g + 4, :].rearrange("p h n -> p (h n)")
                v.scalar_tensor_tensor(y, tanh_c[:, :], 1.0, y, ALU.add, ALU.mult).then_inc(qkv_ready[g], 1)

            def gate(t, p, fl):
                done(dve, tanh_za_ready if fl == FILL_ZA else tanh_zb_ready, t)
                dst = gate_a[p] if fl == FILL_ZA else gate_b
                v.scalar_tensor_tensor(dst, tanh_z[:, :].rearrange("p (h n) -> p h n", h=4), 1.0,
                                       heads((p + fl) % 2), ALU.add, ALU.mult).then_inc(
                    gate_a_ready if fl == FILL_ZA else gate_b_ready, 1)

            def gates(t):
                count = 0

                def link(ins):
                    nonlocal count
                    count += 1
                    ins.then_inc(gate_link, 1)

                def linked():
                    dve.wait_ge(gate_link, t * GATE_LINKS + count)

                u, a, z, z2 = gtmp
                done(dve, ab_ready, t)
                link(v.tensor_tensor(u, ab[:, 4:8], dt_bias, ALU.add))
                linked()
                v.scalar_tensor_tensor(soft_arg, u, -1.0, u, ALU.mult, ALU.min).then_inc(soft_arg_ready, 1)
                yield
                done(dve, soft_exp_ready, t)
                v.tensor_scalar(beta, beta_tanh, 1.0, 0.5, ALU.add, ALU.mult)
                link(v.tensor_scalar(a, soft_exp, 2.0, None, ALU.add))
                yield
                linked()
                link(v.reciprocal(z2, a))
                yield
                linked()
                link(v.tensor_tensor(z, soft_exp, z2, ALU.mult))
                yield
                linked()
                link(v.tensor_tensor(z2, z, z, ALU.mult))
                yield
                linked()
                link(v.tensor_scalar(a, z2, SERIES[7], None, ALU.mult))
                yield
                for n in (6, 5, 4, 3, 2, 1):
                    linked()
                    link(v.scalar_tensor_tensor(a, a, SERIES[n], z2, ALU.add, ALU.mult))
                    yield
                linked()
                link(v.tensor_scalar(a, a, SERIES[0], None, ALU.add))
                yield
                linked()
                link(v.scalar_tensor_tensor(z, a, 2.0, z, ALU.mult, ALU.mult))
                yield
                linked()
                link(v.scalar_tensor_tensor(a, u, 0.0, z, ALU.max, ALU.add))
                yield
                linked()
                v.tensor_tensor(g_tok, a, neg_a, ALU.mult).then_inc(g_ready, 1)
                assert count == GATE_LINKS

            def step(t, p, mix, proj, prep):
                m = t - 1
                first = isinstance(m, int) and m == 0

                def couple(lv):
                    done(dve, p_turn[lv], m)
                    if lv == LEVELS - 1:
                        v.tensor_copy(prod[64:128, :, 0:64], bank[2][64:128, 0:256].rearrange(
                            "p (h n) -> p h n", h=4)).then_inc(p_ready[lv].sem, 1)
                        return
                    v.tensor_tensor(halves(prod[:, :, :], lv, 0), packed(2, 0, lv), mask_halves(masks[:, lv, :], lv, 0),
                                    ALU.mult).then_inc(p_ready[lv].sem, 1)

                def update(lv):
                    done(dve, tp_turn[lv], m)
                    dst = halves(inv_t[:, :, :], lv, 0)
                    v.tensor_tensor(dst, dst, packed(2, 256, lv), ALU.subtract).then_inc(t_ready[lv].sem, 1)

                gate_steps = gates(t) if proj else None
                if mix:
                    done(dve, g_row_t, m)
                    done(dve, exp_cols_ready, m - 1)
                    v.tensor_copy(g_cols[:, 8:12], heads(2)[:, :, TOK - 1])
                    done(dve, g_col_t, m)
                    v.tensor_copy(g_cols[:, 0:4], bank[3][:, 0:4]).then_inc(g_cols_used, 1)
                    done(dve, g_cols_used, m)
                    v.tensor_tensor(g_cols[:, 4:8], g_cols[:, 8:12], g_cols[:, 0:4], ALU.subtract)
                    done(dve, aw_ready, m - 1)
                    for h in range(4):
                        last = v.scalar_tensor_tensor(decay[:, h, :], heads(2)[:, h, :], g_cols[:, h:h + 1], neg,
                                                      ALU.subtract, ALU.add)
                    last.then_inc(decay_arg_ready, 1)
                    if first:
                        dve.wait_ge(pw_loaded, 16)
                        v.tensor_scalar(post_w, post_w, D ** 0.5, None, ALU.mult).then_inc(post_w_ready, 1)
                        dve.wait_ge(post_w_ready, 1)
                    else:
                        finish(m - 1)
                    done(dve, k_sq_ready, m)
                    v.tensor_reduce(norms[:, 0:4], prod[:, :, :], AX_X, ALU.add).then_inc(k_sq_used, 1)
                    done(dve, k_sq_used, m)
                    v.tensor_scalar(norms[:, 0:4], norms[:, 0:4], 0.25, EPS, ALU.mult, ALU.add).then_inc(k_norms_ready, 1)
                    done(dve, k_norms_ready, m)
                    v.reciprocal(key_inv, norms[:, 0:4]).then_inc(norm_link, 1)
                    dve.wait_ge(norm_link, m * 3 + 1)
                    done(dve, g_ready, m)
                    v.scalar_tensor_tensor(key_c, key_inv, 0.25, beta, ALU.mult, ALU.mult).then_inc(norm_link, 1)
                    dve.wait_ge(norm_link, m * 3 + 2)
                    v.tensor_scalar(key_nc, key_c, -1.0, None, ALU.mult)
                    done(dve, Nth(gram_t, 2, 0), m)
                    done(dve, decay_ready, m)
                    done(dve, o_turned, m - 1)
                    for h in range(4):
                        last = v.scalar_tensor_tensor(mt[:, h, :], heads(4)[:, h, :], key_c[:, h:h + 1],
                                                      decay[:, h, :], ALU.mult, ALU.mult)
                    last.then_inc(m_ready, 1)
                    done(dve, m_ready, m)
                    v.tensor_tensor(halves(prod[:, :, :], 0, 1), halves(mt[:, :, :], 0, 1),
                                    mask_halves(masks[:, 0, :], 0, 1), ALU.mult).then_inc(c0_ready, 1)
                    done(dve, c0_ready, m)
                    v.tensor_tensor(halves(inv_u[:, :, :], 0, 1), mask_halves(ident, 0, 1),
                                    halves(prod[:, :, :], 0, 1), ALU.subtract).then_inc(u0_ready, 1)
                    done(dve, Nth(gram_t, 2, 1), m)
                    v.tensor_tensor(decay[:, :, :], heads(5), decay[:, :, :], ALU.mult).then_inc(at_ready, 1)
                    done(dve, sq_ready, m)
                    v.tensor_reduce(norms[:, 4:8], k_tail, AX_X, ALU.add).then_inc(norm_link, 1)
                    dve.wait_ge(norm_link, m * 3 + 3)
                    v.tensor_scalar(norms[:, 4:8], norms[:, 4:8], 0.25, EPS, ALU.mult, ALU.add).then_inc(norms_ready, 1)
                    done(dve, exp_cols_ready, m)
                    v.tensor_tensor(k_tail, heads(6), bc(exp_cols[:, 4:8], 128), ALU.mult).then_inc(k_tail_ready, 1)
                if proj:
                    gate(t, p, FILL_ZA)
                    if not mix:
                        w_out_low(0)
                if mix:
                    done(dve, v_turned, m)
                    done(dve, key_norm_ready, m)
                    done(dve, w_mm_ready, m - 1)
                    v.tensor_tensor(rhs[:, :, :], heads(7), bc(key_norm, 128), ALU.mult).then_inc(vn_ready, 1)
                if mix:
                    done(dve, scores_ready, m)
                    if first:
                        for b in (4, 5):
                            last = v.memset(heads(b)[0:64, :, 0:64], NEG)
                        last.then_inc(no_chunk, 1)
                        dve.wait_ge(no_chunk, 1)
                    for half in range(2):
                        last = v.tensor_reduce(row_max[:, 4 * half:4 * half + 4], heads(4 + half), AX_X, ALU.max)
                    last.then_inc(soft_link, 1)
                    couple(1)
                    dve.wait_ge(soft_link, m * 5 + 1)
                    v.tensor_tensor(row_max, row_max, sinks8, ALU.max).then_inc(soft_link, 1)
                    dve.wait_ge(soft_link, m * 5 + 2)
                    v.tensor_tensor(sink_arg, sinks8, row_max, ALU.subtract)
                    done(dve, post_ready, m - 1)
                    for half in range(2):
                        last = v.tensor_tensor(soft[:, 4 * half:4 * half + 4, :], heads(4 + half),
                                               bc(row_max[:, 4 * half:4 * half + 4], 128), ALU.subtract)
                    last.then_inc(sub_ready, 1)
                    update(1)
                if proj:
                    convolve(t, FILL_V, [0], v_turned if mix else None, m)
                    if not mix:
                        w_out_low(1)
                if mix:
                    couple(2)
                    done(dve, exp_ready, m)
                    v.tensor_reduce(row_sum, soft[:, :, :], AX_X, ALU.add).then_inc(soft_link, 1)
                    dve.wait_ge(soft_link, m * 5 + 3)
                    v.tensor_tensor(row_sum, row_sum, sink_arg, ALU.add).then_inc(soft_link, 1)
                    dve.wait_ge(soft_link, m * 5 + 4)
                    v.reciprocal(row_max, row_sum).then_inc(soft_link, 1)
                    dve.wait_ge(soft_link, m * 5 + 5)
                    v.tensor_scalar(row_sum, row_max, out_f, None, ALU.mult).then_inc(rsum_ready, 1)
                    update(2)
                if proj:
                    convolve(t, FILL_V, [1])
                    next(gate_steps)
                if mix:
                    couple(3)
                    done(dve, ks_ready, m)
                    for h in range(4):
                        last = v.scalar_tensor_tensor(rhs[:, h, :], heads(7)[:, h, :], exp_cols[:, h:h + 1],
                                                      rhs[:, h, :], ALU.mult, ALU.subtract)
                    last.then_inc(rhs_ready, 1)
                    update(3)
                if proj:
                    convolve(t, FILL_V, [2])
                if mix:
                    couple(4)
                    done(dve, pv_ready, m)
                    done(dve, y_ready, m - 1)
                    v.tensor_tensor(heads(6), heads(6), gate_b, ALU.mult).then_inc(out_b_raw, 1)
                    update(4)
                if proj:
                    convolve(t, FILL_V, [3], between=gate_steps)
                if mix:
                    couple(5)
                if proj:
                    silu(t, 2)
                if mix:
                    update(5)
                if proj:
                    convolve(t, FILL_K, [0], ks_ready if mix else None, m, gate_steps)
                if mix:
                    couple(6)
                    done(dve, out_b_high, m)
                    v.tensor_tensor(out_b_half[:, 1, :, :], heads(6), out_b_half[:, 0, :, :],
                                    ALU.subtract).then_inc(out_b_ready, 1)
                if mix:
                    done(dve, up_turn, m)
                    dst = inv_u[0:64, :, 64:128]
                    v.tensor_tensor(dst, dst, bank[3][0:64, 0:256].rearrange("p (h n) -> p h n", h=4),
                                    ALU.subtract).then_inc(inverse_ready, 1)
                if proj:
                    convolve(t, FILL_K, [1], between=gate_steps)
                if mix:
                    done(dve, w_mm_ready, m)
                    v.tensor_tensor(cw[:, :, :], heads(6), bc(key_nc, 128), ALU.mult).then_inc(w_ready, 1)
                    done(dve, qs_ready, m)
                    v.tensor_tensor(mt[:, :, :], heads(3), bc(exp_cols[:, 0:4], 128), ALU.mult).then_inc(qs_used, 1)
                if proj:
                    convolve(t, FILL_K, [2], between=gate_steps)
                    for _ in gate_steps:
                        pass
                if mix:
                    done(dve, aw_ready, m)
                    done(dve, qs_used, m)
                    v.tensor_tensor(mt[:, :, :], mt[:, :, :], heads(7), ALU.add).then_inc(o_ready, 1)
                    for h in range(4):
                        last = v.scalar_tensor_tensor(state[:, h, :], state[:, h, :], exp_cols[:, 8 + h:9 + h],
                                                      heads(2)[:, h, :], ALU.mult, ALU.add)
                    last.then_inc(state_ready, 1)
                if mix:
                    done(dve, o_sq_ready, m)
                    v.tensor_scalar(o_arg, o_sq, 1.0 / 128, None, ALU.mult).then_inc(o_link, 1)
                    done(dve, o_link, m)
                    v.scalar_tensor_tensor(o_arg, norms[:, 4:8], EPS * 4 * 128, o_arg, ALU.mult, ALU.add).then_inc(
                        o_arg_ready, 1)
                if proj:
                    convolve(t, FILL_K, [3])
                if prep:
                    low_half(t + 1)
                if proj:
                    gate(t, p, FILL_ZB)
                    if not mix:
                        w_out_low(2)
                if mix:
                    done(dve, o_turned, m)
                    v.tensor_tensor(heads(3), heads(3), gate_a[1 - p], ALU.mult).then_inc(out_a_raw, 1)
                if proj:
                    silu(t, 1)
                if mix:
                    done(dve, out_a_high, m)
                    v.tensor_tensor(out_a_half[:, 1, :, :], heads(3), out_a_half[:, 0, :, :],
                                    ALU.subtract).then_inc(out_a_ready, 1)
                if prep:
                    copy_xt(t + 1, True)
                if proj:
                    convolve(t, FILL_Q, range(4), qs_ready if mix else None, m)
                    silu(t, 0)
                    if not mix:
                        w_out_low(3)

            def finish(m):
                done(dve, y_rs_ready, m)
                for n in range(2):
                    last = v.scalar_tensor_tensor(shared[:, 512 * n:512 * n + 512], bank[4 + n][:, :], y_rs,
                                                  post_w[:, 512 * n:512 * n + 512], ALU.mult, ALU.mult)
                last.then_inc(y_used, 1)

            for c in range(NC):
                dve.wait_ge(w_loaded[c], 64)
                if c == 3:
                    low_half(0)
                    copy_xt(0, False)
                last = v.tensor_reduce(w_max[:, c:c + 1], w_raw[:, c + 1, :], AX_X, ALU.max,
                                       apply_absolute_value=True)
            last.then_inc(setup_link, 1)
            dve.wait_ge(setup_link, 2)
            v.tensor_tensor(w_max, w_max, cols[:, 48:56], ALU.mult).then_inc(setup_link, 1)
            dve.wait_ge(setup_link, 3)
            v.tensor_reduce(w_amax[:, 0:1], w_max, AX_X, ALU.max, apply_absolute_value=True).then_inc(w_max_ready, 1)
            v.tensor_tensor(w_sq, w_max, w_max, ALU.mult).then_inc(w_sq_link, 1)
            dve.wait_ge(w_sq_link, 1)
            v.tensor_reduce(w_sum, w_sq, AX_X, ALU.add).then_inc(w_sum_ready, 1)
            dve.wait_ge(w_amax_ready, 1)
            v.tensor_scalar(w_amax[:, 0:1], w_amax[:, 1:2], 1e-30, None, ALU.max).then_inc(setup_link, 1)
            dve.wait_ge(setup_link, 4)
            v.tensor_single_scalar(w_pow2.bitcast(I32), w_amax[:, 0:1].bitcast(I32), 0x7F800000,
                                   ALU.bitwise_and).then_inc(setup_link, 1)
            dve.wait_ge(setup_link, 5)
            v.reciprocal(w_scale, w_pow2).then_inc(setup_link, 1)
            dve.wait_ge(setup_link, 6)
            v.tensor_scalar(row_scale, cols[:, 48:56], w_scale, 2.0 ** 14, ALU.mult, ALU.mult).then_inc(w_scale_ready, 1)
            v.tensor_scalar(unscale, w_pow2, 2.0 ** -14 / X_SCALE, None, ALU.mult)
            v.tensor_scalar(half_unscale, w_pow2, 2.0 ** -15 / X_SCALE, None, ALU.mult).then_inc(setup_link, 1)
            dve.wait_ge(setup_link, 7)
            v.tensor_scalar(conv_taps, conv_taps, unscale, None, ALU.mult)
            dve.wait_ge(w_total_ready, 1)
            v.tensor_scalar(mix_bound, w_total, float(D), 128.0, ALU.mult, ALU.max).then_inc(setup_link, 1)
            dve.wait_ge(setup_link, 8)
            v.reciprocal(mix_f, mix_bound).then_inc(setup_link, 1)
            dve.wait_ge(setup_link, 9)
            v.scalar_tensor_tensor(out_f, mix_f, MIX_TOP, half_unscale, ALU.mult, ALU.mult)
            for c in range(NC):
                for part in range(2):
                    dve.wait_ge(w_hi_ready, 2 * c + part + 1)
                    if c == 0:
                        dve.wait_ge(w_scale_ready, 1)
                    elif part == 0:
                        dve.wait_ge(w_lo_ready, 2 * c)
                    r = slice(COLS // 2 * part, COLS // 2 * part + COLS // 2)
                    v.scalar_tensor_tensor(w_half[:, c, 1, r], w_raw[:, c + 1, r], row_scale[:, c:c + 1],
                                           w_half[:, c, 0, r], ALU.mult, ALU.subtract).then_inc(w_lo_ready, 1)
            dve.wait_ge(wo_loaded, 16 * NC)
            for c in range(NC):
                last = v.tensor_reduce(wo_max[:, c:c + 1], w_o[:, c, :], AX_X, ALU.max, apply_absolute_value=True)
            last.then_inc(setup_link, 1)
            dve.wait_ge(setup_link, 10)
            v.tensor_scalar(wo_max[:, 0:4], wo_max[:, 0:4], cols[:, 56:57], None, ALU.mult).then_inc(setup_link, 1)
            dve.wait_ge(setup_link, 11)
            v.tensor_reduce(wo_amax[:, 0:1], wo_max, AX_X, ALU.max, apply_absolute_value=True).then_inc(wo_max_ready, 1)
            dve.wait_ge(wo_amax_ready, 1)
            v.tensor_scalar(wo_amax[:, 0:1], wo_amax[:, 1:2], 1e-9, None, ALU.max).then_inc(setup_link, 1)
            dve.wait_ge(setup_link, 12)
            v.tensor_single_scalar(wo_pow2.bitcast(I32), wo_amax[:, 0:1].bitcast(I32), 0x7F800000,
                                   ALU.bitwise_and).then_inc(setup_link, 1)
            dve.wait_ge(setup_link, 13)
            v.reciprocal(wo_amax[:, 1:2], wo_pow2).then_inc(setup_link, 1)
            dve.wait_ge(setup_link, 14)
            v.tensor_scalar(wo_scale[:, 1:2], wo_amax[:, 1:2], 2.0 ** 14, None, ALU.mult).then_inc(setup_link, 1)
            dve.wait_ge(setup_link, 15)
            v.tensor_tensor(wo_scale[:, 0:1], wo_scale[:, 1:2], cols[:, 56:57], ALU.mult).then_inc(wo_scale_ready, 1)
            v.scalar_tensor_tensor(mix_f, mix_f, MIX_TOP, wo_scale[:, 1:2], ALU.mult, ALU.mult).then_inc(setup_link, 1)
            dve.wait_ge(setup_link, 16)
            v.scalar_tensor_tensor(eps_y, mix_f, D * EPS, mix_f, ALU.mult, ALU.mult)
            run_steps(dve, step)
            finish(NT - 1)

        @block.gpsimd
        def _(pool):
            g = nc.gpsimd
            g.memset(power[:, 0:8], -0.5)
            g.memset(eps_sum, D * EPS)
            g.memset(root_scale, X_SCALE * D ** 0.5)
            g.memset(power[:, 8:16], 0.5).then_inc(pool_set, 1)
            pool.wait_ge(pool_set, 1)

            def rotate(dst, src, swap, n):
                cos, sin = rot_tab[:, 0:64], rot_tab[:, 64:128]
                g.tensor_tensor(dst, src, over_heads(cos, n), ALU.mult)
                for h in range(2):
                    last = g.tensor_tensor(swap[:, :, 32 * h:32 * h + 32], src[:, :, 32 - 32 * h:64 - 32 * h],
                                           over_heads(sin[:, 32 * h:32 * h + 32], n), ALU.mult)
                return last

            def step(t, p, mix, proj, prep):
                m = t - 1

                if mix:
                    done(pool, w_mm_ready, m - 1)
                    g.tensor_tensor(halves(inv_u[:, :, :], 0, 0), mask_halves(ident, 0, 0), mask_halves(ident, 0, 0),
                                    ALU.mult).then_inc(u0_blank, 1)
                    if not (isinstance(m, int) and m == 0):
                        post(m - 1)
                    done(pool, k_norms_ready, m)
                    g.tensor_tensor(key_norm, norms[:, 0:4], power[:, 8:12], ALU.pow).then_inc(key_norm_ready, 1)
                    done(pool, rsum_ready, m)
                    g.tensor_tensor(soft[:, :, :], soft[:, :, :], bc(row_sum, 128), ALU.mult).then_inc(soft_ready, 1)
                if proj:
                    pool.wait_ge(rot_loaded, (t + 1) * 16)
                    done(pool, kv_raw_ready, t)
                    if mix:
                        done(pool, kr_turned, m)
                    rotate(k_rot[:, :, 0, :], k_raw[:, :, :], k_sw[:, :, :], 2).then_inc(rot_link, 1)
                    pool.wait_ge(rot_link, t * 2 + 1)
                    g.tensor_tensor(k_rot[:, :, 1, :], k_rot[:, :, 0, :], k_sw[:, :, :], ALU.add)
                    g.tensor_tensor(k_rot[:, :, 0, :], k_rot[:, :, 0, :], k_sw[:, :, :], ALU.add).then_inc(k_rot_ready, 1)
                if proj:
                    done(pool, q_raw_ready, t)
                    if mix:
                        done(pool, scores_ready, m)
                    q8 = q_rot[:, :].rearrange("p (h n) -> p h n", h=8)
                    rotate(q8, rot_in, rot_sw, 8).then_inc(rot_link, 1)
                    pool.wait_ge(rot_link, t * 2 + 2)
                    g.tensor_tensor(q8, q8, rot_sw, ALU.add).then_inc(q_rot_ready, 1)
                if mix:
                    done(pool, tp_turn[LEVELS - 2], m)
                    g.tensor_tensor(prod[0:64, :, 0:64], over_heads(ident, 4)[0:64, :, 0:64],
                                    over_heads(ident, 4)[0:64, :, 0:64], ALU.subtract).then_inc(p_clear, 1)
                if prep:
                    root_x(t + 1)
                if mix:
                    done(pool, o_arg_ready, m)
                    g.tensor_tensor(o_f, o_arg, power[:, 0:4], ALU.pow).then_inc(o_f_ready, 1)
                    done(pool, o_f_ready, m)
                    g.tensor_tensor(o_f, o_f, out_f.broadcast_to([128, 4]), ALU.mult).then_inc(pool_link, 1)
                    pool.wait_ge(pool_link, m * 3 + 1)
                    g.tensor_tensor(mt[:, :, :], mt[:, :, :], bc(o_f, 128), ALU.mult).then_inc(on_ready, 1)
                    done(pool, y_sq_ready, m)
                    g.tensor_tensor(y_arg, y_sq[:, 0:1], y_sq[:, 1:2], ALU.add).then_inc(pool_link, 1)
                    pool.wait_ge(pool_link, m * 3 + 2)
                    g.tensor_tensor(y_arg, y_arg, eps_y, ALU.add).then_inc(pool_link, 1)
                    pool.wait_ge(pool_link, m * 3 + 3)
                    g.tensor_tensor(y_rs, y_arg, power[:, 0:1], ALU.pow).then_inc(y_rs_ready, 1)

            def post(m):
                done(pool, y_used, m)
                pool.wait_ge(res_loaded, (m + 1) * 16)
                g.tensor_tensor(y_out[:, :], y_out[:, :], shared[:, :], ALU.add).then_inc(post_ready, 1)

            def root_x(n):
                done(pool, x_sq_ready, n)
                g.tensor_tensor(x_arg, x_sq, eps_sum, ALU.add).then_inc(x_link, 1)
                done(pool, Nth(x_link, 2, 0), n)
                g.tensor_tensor(x_arg, x_arg, power[:, 0:1], ALU.pow).then_inc(x_link, 1)
                done(pool, Nth(x_link, 2, 1), n)
                g.tensor_tensor(x_rs, x_arg, root_scale, ALU.mult).then_inc(x_rs_ready, 1)

            root_x(0)
            pool.wait_ge(w_max_ready, 1)
            g.partition_all_reduce(w_amax[:, 1:2], w_amax[:, 0:1], 128, RMAX).then_inc(w_amax_ready, 1)
            pool.wait_ge(w_sum_ready, 1)
            g.partition_all_reduce(w_total, w_sum, 128, RSUM).then_inc(w_total_ready, 1)
            pool.wait_ge(wo_max_ready, 1)
            g.partition_all_reduce(wo_amax[:, 1:2], wo_amax[:, 0:1], 128, RMAX).then_inc(wo_amax_ready, 1)
            run_steps(pool, step)
            post(NT - 1)


_INS = ["x", "pre_norm_w", "w_in", "conv_w", "dn_a_log", "dn_dt_bias", "dn_out_norm_w", "sw_sinks", "w_out",
        "post_norm_w"]


def _constants(seq):
    import numpy as np

    n = TOK
    at = np.arange(n)
    ident = np.eye(n, dtype=np.float32)
    upper = (at[:, None] <= at[None, :]).astype(np.float32)
    neg = np.where(at[:, None] <= at[None, :], 0.0, NEG).astype(np.float32)
    const32 = np.ascontiguousarray(np.stack([ident, upper, neg], 1))
    masks = []
    row, col = at[:, None], at[None, :]
    for lv in range(LEVELS - 1):
        m = 2 ** lv
        masks.append((col // (2 * m) == row // (2 * m)) & (col // m % 2 == 0) & (row // m % 2 == 1))
    const16 = np.ascontiguousarray(np.stack([masks[0].T] + masks[1:] + [np.eye(n, dtype=bool)], 1).astype(np.float16))
    half = DH_B // 2
    freq = (10000.0 ** (-np.arange(half) * 2.0 / DH_B)).astype(np.float32)
    ang = (np.arange(seq, dtype=np.float32)[:, None] * freq[None, :]).astype(np.float64)
    rotary = np.concatenate([np.cos(ang), np.cos(ang), -np.sin(ang), np.sin(ang)], 1).astype(np.float32)
    return {"const32": const32, "const16": const16, "rotary": rotary}


def kernel(**inputs):
    import numpy as np
    import concourse.bacc as bacc
    from concourse.bass_utils import run_bass_kernel_spmd as run

    nc = bacc.Bacc("TRN2", target_bir_lowering=False, num_devices=1)
    data = {name: np.ascontiguousarray(inputs[name]) for name in _INS}
    data.update(_constants(inputs["x"].shape[1]))
    arrays, args = {}, []
    for name, a in data.items():
        arrays[f"in_{name}_dram"] = a
        args.append(nc.dram_tensor(f"in_{name}_dram", a.shape, mybir.dt.from_np(a.dtype), kind="ExternalInput").ap())
    args.append(nc.dram_tensor("out_0_dram", data["x"].shape, F32, kind="ExternalOutput").ap())
    build(nc, *args)
    r = run(nc, [arrays], core_ids=[0])
    return r.results[0]["out_0_dram"]
```
